# Optimizing a Trainium2 kernel written in Bass

```python
import math
import jax, jax.numpy as jnp
from jax import lax
import numpy as np

D_MODEL = 1024
BATCH = 1
SEQ = 2048
DEPTH = 2

GRID_W = 64
CTX_LEN = 256
EPS = 1e-6

GDN_QK_HEADS = 8
GDN_V_HEADS = 16
GDN_HEAD_DIM = 128
GDN_QK_W = GDN_QK_HEADS * GDN_HEAD_DIM
GDN_V_W = GDN_V_HEADS * GDN_HEAD_DIM
GDN_QKV_W = 2 * GDN_QK_W + GDN_V_W
GDN_IN_W = GDN_QKV_W + GDN_V_W + 4 * GDN_V_HEADS
GDN_CHUNK = 64

LRU_W = D_MODEL
LRU_BLOCKS = 4
LRU_BS = LRU_W // LRU_BLOCKS
RG_C = 8.0

CONV_W = 4
CONV_LEFT = 2

N_GDN = (DEPTH + 1) // 2
N_LRU = DEPTH // 2

kernel_name = "hybrid_gdn_rglru_prefix_dit"

def rmsnorm(x, g):
    xf = x.astype(jnp.float32)
    y = xf * lax.rsqrt(jnp.mean(xf * xf, axis=-1, keepdims=True) + EPS)
    return y.astype(x.dtype) * g

def l2norm(x):
    xf = x.astype(jnp.float32)
    return (xf * lax.rsqrt(jnp.sum(xf * xf, axis=-1, keepdims=True) + EPS)).astype(x.dtype)

def short_conv(x, w):
    T = x.shape[1]
    xp = jnp.pad(x, ((0, 0), (CONV_LEFT, CONV_W - 1 - CONV_LEFT), (0, 0)))
    out = xp[:, 0:T] * w[0]
    for j in range(1, CONV_W):
        out = out + xp[:, j:j + T] * w[j]
    return out

def to_col_major(t, rows):
    B, T, D = t.shape
    return t.reshape(B, rows, GRID_W, D).transpose(0, 2, 1, 3).reshape(B, T, D)

def from_col_major(t, rows):
    B, T, D = t.shape
    return t.reshape(B, GRID_W, rows, D).transpose(0, 2, 1, 3).reshape(B, T, D)

def chunk_gated_delta(q, k, v, g, beta, s0):
    out_dtype = v.dtype
    q, k, v, g, beta = (t.astype(jnp.float32) for t in (q, k, v, g, beta))
    B, T, H, DK = q.shape
    DV = v.shape[-1]
    C = GDN_CHUNK
    N = T // C
    ch = lambda t: t.reshape(B, N, C, H, -1).transpose(0, 3, 1, 2, 4)
    q, k, v = ch(q), ch(k), ch(v)
    g = g.reshape(B, N, C, H).transpose(0, 3, 1, 2)
    beta = beta.reshape(B, N, C, H).transpose(0, 3, 1, 2)
    g = jnp.cumsum(g, axis=-1)
    tril = jnp.tril(jnp.ones((C, C), bool))
    strict = jnp.tril(jnp.ones((C, C), bool), -1)
    diff = g[..., :, None] - g[..., None, :]
    decay = jnp.where(tril, jnp.exp(jnp.where(tril, diff, 0.0)), 0.0)
    kb = k * beta[..., None]
    L = jnp.where(strict, jnp.einsum('bhncd,bhnsd->bhncs', kb, k) * decay, 0.0)
    eye = jnp.eye(C, dtype=jnp.float32)
    rhs = jnp.concatenate([v * beta[..., None], kb * jnp.exp(g)[..., None]], axis=-1)
    sol = lax.linalg.triangular_solve(eye + L, rhs, left_side=True, lower=True, unit_diagonal=True)
    u, w = sol[..., :DV], sol[..., DV:]
    qk = jnp.where(tril, jnp.einsum('bhncd,bhnsd->bhncs', q, k) * decay, 0.0)
    q_dec = q * jnp.exp(g)[..., None]
    k_dec = k * jnp.exp(g[..., -1:] - g)[..., None]
    g_last = jnp.exp(g[..., -1])

    def step(S, xs):
        qk_i, u_i, w_i, qd_i, kd_i, gl_i = xs
        v_new = u_i - jnp.einsum('bhcd,bhde->bhce', w_i, S)
        o = jnp.einsum('bhcd,bhde->bhce', qd_i, S) + jnp.einsum('bhcs,bhse->bhce', qk_i, v_new)
        S = S * gl_i[..., None, None] + jnp.einsum('bhcd,bhce->bhde', kd_i, v_new)
        return S, o

    xs = tuple(jnp.moveaxis(t, 2, 0) for t in (qk, u, w, q_dec, k_dec, g_last))
    S, o = lax.scan(step, s0.astype(jnp.float32), xs)
    o = o.transpose(1, 0, 3, 2, 4).reshape(B, T, H, DV)
    return o.astype(out_dtype), S

def gdn_sequence(h, w_in, conv_w, a_log, dt_bias, norm_g, w_out, s0):
    B, T, _ = h.shape
    proj = h @ w_in
    qkv, z, ab = jnp.split(proj, [GDN_QKV_W, GDN_QKV_W + GDN_V_W], axis=-1)
    qkv = jax.nn.silu(short_conv(qkv, conv_w))
    q, k, v = jnp.split(qkv, [GDN_QK_W, 2 * GDN_QK_W], axis=-1)
    rep = GDN_V_HEADS // GDN_QK_HEADS
    q = jnp.repeat(l2norm(q.reshape(B, T, GDN_QK_HEADS, GDN_HEAD_DIM)) * (GDN_HEAD_DIM ** -0.5), rep, axis=2)
    k = jnp.repeat(l2norm(k.reshape(B, T, GDN_QK_HEADS, GDN_HEAD_DIM)), rep, axis=2)
    v = v.reshape(B, T, GDN_V_HEADS, GDN_HEAD_DIM)
    ab = ab.reshape(B, T, 2, 2, GDN_V_HEADS).astype(jnp.float32)
    g = -jnp.exp(a_log) * jax.nn.softplus(ab[..., 0, :] + dt_bias)
    beta = jax.nn.sigmoid(ab[..., 1, :])
    o_f, s_f = chunk_gated_delta(q, k, v, g[:, :, 0], beta[:, :, 0], s0[0])
    fl = lambda t: jnp.flip(t, axis=1)
    o_b, s_b = chunk_gated_delta(fl(q), fl(k), fl(v), fl(g[:, :, 1]), fl(beta[:, :, 1]), s0[1])
    o = o_f + fl(o_b)
    o = rmsnorm(o, norm_g) * jax.nn.silu(z).reshape(B, T, GDN_V_HEADS, GDN_HEAD_DIM)
    y = o.reshape(B, T, GDN_V_W) @ w_out
    return y, jnp.stack([s_f, s_b])

def gdn_mixer(h_ctx, h_lat, w_in, conv_w, a_log, dt_bias, norm_g, w_out):
    B = h_ctx.shape[0]
    s0 = jnp.zeros((2, B, GDN_V_HEADS, GDN_HEAD_DIM, GDN_HEAD_DIM), jnp.float32)
    y_ctx, s_ctx = gdn_sequence(h_ctx, w_in, conv_w, a_log, dt_bias, norm_g, w_out, s0)
    y_lat, _ = gdn_sequence(h_lat, w_in, conv_w, a_log, dt_bias, norm_g, w_out, s_ctx)
    return y_ctx, y_lat

def linear_scan(a, b, h0):
    def combine(l, r):
        return (l[0] * r[0], r[0] * l[1] + r[1])
    a_cum, h = lax.associative_scan(combine, (a, b), axis=1)
    return a_cum * h0[:, None] + h

def rglru_sequence(h, w_in, conv_w, conv_b, w_r, b_r, w_i, b_i, lam, w_out, h0):
    B, T, _ = h.shape
    xb, gate = jnp.split(h @ w_in, [LRU_W], axis=-1)
    xc = short_conv(xb, conv_w) + conv_b
    xblk = xc.reshape(B, T, LRU_BLOCKS, LRU_BS)
    r = jax.nn.sigmoid(jnp.einsum('btnc,dncs->btdns', xblk, w_r).reshape(B, T, 2, LRU_W) + b_r)
    i = jax.nn.sigmoid(jnp.einsum('btnc,dncs->btdns', xblk, w_i).reshape(B, T, 2, LRU_W) + b_i)
    log_a = -RG_C * r.astype(jnp.float32) * jax.nn.softplus(-lam.astype(jnp.float32))
    a = jnp.exp(log_a)
    b = jnp.sqrt(-jnp.expm1(2.0 * log_a)) * (i.astype(jnp.float32) * xc.astype(jnp.float32)[:, :, None])
    h_f = linear_scan(a[:, :, 0], b[:, :, 0], h0[0])
    h_b = jnp.flip(linear_scan(jnp.flip(a[:, :, 1], 1), jnp.flip(b[:, :, 1], 1), h0[1]), 1)
    y = ((h_f + h_b).astype(h.dtype) * jax.nn.silu(gate)) @ w_out
    return y, jnp.stack([h_f[:, -1], h_b[:, 0]])

def rglru_mixer(h_ctx, h_lat, w_in, conv_w, conv_b, w_r, b_r, w_i, b_i, lam, w_out):
    B = h_ctx.shape[0]
    h0 = jnp.zeros((2, B, LRU_W), jnp.float32)
    y_ctx, h_ctx_state = rglru_sequence(h_ctx, w_in, conv_w, conv_b, w_r, b_r, w_i, b_i, lam, w_out, h0)
    y_lat, _ = rglru_sequence(h_lat, w_in, conv_w, conv_b, w_r, b_r, w_i, b_i, lam, w_out, h_ctx_state)
    return y_ctx, y_lat

def setup_inputs(seed: int = 0) -> dict:
    key = jax.random.key(seed)
    ks = jax.random.split(key, 24)
    nrm = lambda k, shape, s: jax.random.normal(k, shape, jnp.float32) * s
    x = nrm(ks[0], (BATCH, SEQ, D_MODEL), 1.0)
    c = nrm(ks[1], (BATCH, D_MODEL), 1.0)
    ctx = nrm(ks[2], (BATCH, CTX_LEN, D_MODEL), 1.0)
    c_ctx = nrm(ks[3], (D_MODEL,), 1.0)
    mod_w = nrm(ks[4], (DEPTH, D_MODEL, 3 * D_MODEL), 0.5 * D_MODEL ** -0.5)
    mod_b = nrm(ks[5], (DEPTH, 3 * D_MODEL), 0.02)
    norm_g = 1.0 + nrm(ks[6], (DEPTH, D_MODEL), 0.02)
    gdn_w_in = nrm(ks[7], (N_GDN, D_MODEL, GDN_IN_W), D_MODEL ** -0.5)
    gdn_conv = nrm(ks[8], (N_GDN, CONV_W, GDN_QKV_W), CONV_W ** -0.5)
    gdn_a_log = jnp.log(jax.random.uniform(ks[9], (N_GDN, 2, GDN_V_HEADS), jnp.float32, 1.0, 16.0))
    dt = jnp.exp(jax.random.uniform(ks[10], (N_GDN, 2, GDN_V_HEADS), jnp.float32, math.log(1e-3), math.log(1e-1)))
    gdn_dt_bias = dt + jnp.log(-jnp.expm1(-dt))
    gdn_norm_g = 1.0 + nrm(ks[11], (N_GDN, GDN_HEAD_DIM), 0.02)
    gdn_w_out = nrm(ks[12], (N_GDN, GDN_V_W, D_MODEL), GDN_V_W ** -0.5)
    lru_w_in = nrm(ks[13], (N_LRU, D_MODEL, 2 * LRU_W), D_MODEL ** -0.5)
    lru_conv_w = nrm(ks[14], (N_LRU, CONV_W, LRU_W), CONV_W ** -0.5)
    lru_conv_b = nrm(ks[15], (N_LRU, LRU_W), 0.02)
    lru_w_r = nrm(ks[16], (N_LRU, 2, LRU_BLOCKS, LRU_BS, LRU_BS), LRU_BS ** -0.5)
    lru_b_r = nrm(ks[17], (N_LRU, 2, LRU_W), 0.02)
    lru_w_i = nrm(ks[18], (N_LRU, 2, LRU_BLOCKS, LRU_BS, LRU_BS), LRU_BS ** -0.5)
    lru_b_i = nrm(ks[19], (N_LRU, 2, LRU_W), 0.02)
    a0 = jax.random.uniform(ks[20], (N_LRU, 2, LRU_W), jnp.float32, 0.9, 0.999)
    s = a0 ** (1.0 / RG_C)
    lru_lambda = jnp.log(s) - jnp.log1p(-s)
    lru_w_out = nrm(ks[21], (N_LRU, LRU_W, D_MODEL), LRU_W ** -0.5)
    final_g = 1.0 + nrm(ks[22], (D_MODEL,), 0.02)
    return {"x": x, "c": c, "ctx": ctx, "c_ctx": c_ctx,
            "mod_w": mod_w, "mod_b": mod_b, "norm_g": norm_g,
            "gdn_w_in": gdn_w_in, "gdn_conv": gdn_conv, "gdn_a_log": gdn_a_log,
            "gdn_dt_bias": gdn_dt_bias, "gdn_norm_g": gdn_norm_g, "gdn_w_out": gdn_w_out,
            "lru_w_in": lru_w_in, "lru_conv_w": lru_conv_w, "lru_conv_b": lru_conv_b,
            "lru_w_r": lru_w_r, "lru_b_r": lru_b_r, "lru_w_i": lru_w_i, "lru_b_i": lru_b_i,
            "lru_lambda": lru_lambda, "lru_w_out": lru_w_out, "final_g": final_g}

def reference(x, c, ctx, c_ctx, mod_w, mod_b, norm_g, gdn_w_in, gdn_conv, gdn_a_log, gdn_dt_bias,
              gdn_norm_g, gdn_w_out, lru_w_in, lru_conv_w, lru_conv_b, lru_w_r, lru_b_r, lru_w_i, lru_b_i,
              lru_lambda, lru_w_out, final_g):
    rows = x.shape[1] // GRID_W
    sc = jax.nn.silu(c)
    sc_ctx = jax.nn.silu(c_ctx)
    for i in range(DEPTH):
        shift, scale, gate = jnp.split(sc @ mod_w[i] + mod_b[i], 3, axis=-1)
        shift_c, scale_c, gate_c = jnp.split(sc_ctx @ mod_w[i] + mod_b[i], 3, axis=-1)
        h_lat = rmsnorm(x, norm_g[i]) * (1.0 + scale[:, None]) + shift[:, None]
        h_ctx = rmsnorm(ctx, norm_g[i]) * (1.0 + scale_c) + shift_c
        col_major = (i + i // 2) % 2 == 1
        if col_major:
            h_lat = to_col_major(h_lat, rows)
        j = i // 2
        if i % 2 == 0:
            y_ctx, y_lat = gdn_mixer(h_ctx, h_lat, gdn_w_in[j], gdn_conv[j], gdn_a_log[j],
                                     gdn_dt_bias[j], gdn_norm_g[j], gdn_w_out[j])
        else:
            y_ctx, y_lat = rglru_mixer(h_ctx, h_lat, lru_w_in[j], lru_conv_w[j], lru_conv_b[j],
                                       lru_w_r[j], lru_b_r[j], lru_w_i[j], lru_b_i[j],
                                       lru_lambda[j], lru_w_out[j])
        if col_major:
            y_lat = from_col_major(y_lat, rows)
        x = x + gate[:, None] * y_lat
        if i < DEPTH - 1:
            ctx = ctx + gate_c * y_ctx
    return rmsnorm(x, final_g)


_drawn_inputs = setup_inputs


def setup_inputs(seed=0):
    import zlib

    import numpy as np

    out = dict(_drawn_inputs(seed))
    spreads = {}
    factors = {'ctx': 2.806,
     'norm_g': 4.165,
     'gdn_norm_g': 8.0,
     'lru_b_r': 58.174,
     'lru_b_i': 25.652,
     'final_g': 7.613,
     'lru_conv_b': 5.557}
    for name, (base, spread) in spreads.items():
        noise = np.random.default_rng([zlib.crc32(name.encode()), seed]).standard_normal(out[name].shape)
        drawn = base * np.exp(spread * noise) if base else spread * noise
        out[name] = __import__('jax').numpy.asarray(drawn.astype(out[name].dtype))
    for name, factor in factors.items():
        out[name] = (out[name] * factor).astype(out[name].dtype)
    return out
```

```python
from contextlib import ExitStack

import numpy as np

import concourse.bass as bass
from concourse import mybir

F32 = mybir.dt.float32
F32R = mybir.dt.float32r
F16 = mybir.dt.float16
ACT = mybir.ActivationFunctionType
ALU = mybir.AluOpType
AX = mybir.AxisListType

P = 128
D = 1024
KT = D // P
CTX = 256
SEQ = 2048
GRID_W = 64
ROWS = SEQ // GRID_W
TOK = CTX + SEQ
NCH = TOK // P
CCH = CTX // P
EPS = 1e-6
NQ = 8
NV = 16
HD = 128
BLKS = [(0, CTX)] + [(CTX + 512 * i, 512) for i in range(SEQ // 512)]
NB = len(BLKS)
NLEV = 7
NSTEP = NQ * NCH
RG_C = 8.0
LB = 4
Q_CG, Q_BETA, Q_NBEG, Q_ELG, Q_EL = range(5)
NQTY = 5


def phase_modulation(nc, sem, T, io):
    MT = 3 * KT
    with ExitStack() as ctx:
        sb = lambda n, s, d=F32: ctx.enter_context(nc.sbuf_tensor(n, s, d))
        w = [sb(f"mod_w{l}", [P, KT, 3 * D]) for l in range(2)]
        cvec = sb("cvec", [P, KT, 2])
        sc = sb("silu_c", [P, KT, 2])
        mb = sb("mod_bias", [P, 2, MT])
        ng = sb("norm_g_cols", [P, 2, KT])
        m = sb("mod", [P, 2, MT, 2])
        ps = ctx.enter_context(nc.psum_tensor("mod_ps", [P, 2, MT, 2], F32))
        small, wload, silu, prod, vec = (sem(f"mod_{x}") for x in ("small", "wload", "silu", "prod", "vec"))
        wload1 = sem("mod_wload1")
        with nc.Block() as block:
            @block.sync
            def _(sp):
                sp.dma_start(cvec[:], io["cvec"]).then_inc(small, 16)
                sp.dma_start(mb[:], io["mod_b"]).then_inc(small, 16)
                sp.dma_start(ng[:], io["norm_g"]).then_inc(small, 16)
                sp.dma_start(T["ident"][:], io["ident"]).then_inc(small, 16)
                for l, s in ((0, wload), (1, wload1)):
                    for k in range(KT):
                        sp.dma_start(w[l][:, k, :], io["mod_w"][l, k * P:(k + 1) * P, :]).then_inc(s, 16)

            @block.scalar
            def _(act):
                act.wait_ge(small, 64)
                act.activation(sc[:], cvec[:], ACT.Silu).then_inc(silu, 1)

            @block.tensor
            def _(pe):
                pe.wait_ge(silu, 1)
                for l, s in ((0, wload), (1, wload1)):
                    pe.wait_ge(s, 16 * KT)
                    for mt in range(MT):
                        for k in range(KT):
                            i = pe.matmul(ps[:, l, mt, :], w[l][:, k, mt * P:(mt + 1) * P], sc[:, k, :],
                                          start=(k == 0), stop=(k == KT - 1))
                    i.then_inc(prod, 1)

            @block.vector
            def _(dve):
                coef = T["coef"]
                dve.memset(T["ones"][:], 1.0)
                dve.memset(T["eps"][:], EPS)
                dve.wait_ge(small, 64)
                dve.wait_ge(prod, 2)
                dve.tensor_tensor(m[:], ps[:], mb[:].unsqueeze(3).broadcast_to([P, 2, MT, 2]), ALU.add).then_inc(vec, 1)
                dve.wait_ge(vec, 1)
                for l in range(2):
                    mm = m[:, l].rearrange("p (x k) w -> p x w k", x=3)
                    gb = ng[:, l].unsqueeze(1).broadcast_to([P, 2, KT])
                    dve.tensor_copy(coef[:, l, 1], mm[:, 0])
                    dve.tensor_copy(coef[:, l, 2], mm[:, 2])
                    dve.tensor_scalar(coef[:, l, 0], mm[:, 1], 1.0, None, ALU.add).then_inc(vec, 1)
                    dve.wait_ge(vec, 2 + 2 * l)
                    dve.tensor_tensor(coef[:, l, 0], coef[:, l, 0], gb, ALU.mult).then_inc(vec, 1)
                    dve.wait_ge(vec, 3 + 2 * l)


def phase_norm(nc, sem, T, layer, src, hi, lo, col_major):
    n = f"norm{layer}_"
    with ExitStack() as ctx:
        sb = lambda x, s, d=F32: ctx.enter_context(nc.sbuf_tensor(n + x, s, d))
        xt = [sb(f"x{i}", [P, D]) for i in range(2)]
        xn = [sb(f"xn{i}", [P, D]) for i in range(2)]
        h = [sb(f"h{i}", [P, KT, P]) for i in range(2)]
        ss = [sb(f"ss{i}", [P, 1]) for i in range(2)]
        rt = [sb(f"rt{i}", [P, 1]) for i in range(2)]
        rs = [sb(f"rs{i}", [P, 1]) for i in range(2)]
        tp = [ctx.enter_context(nc.psum_tensor(n + f"tp{i}", [P, KT, P], F32)) for i in range(2)]
        load = [sem(n + f"load{i}") for i in range(2)]
        s_ss, s_rt, s_rs, s_xn, s_tr, s_mul, s_h, s_hi, s_lo = (
            sem(n + x) for x in ("ss", "rt", "rs", "xn", "tr", "mul", "h", "hi", "lo"))

        def place(buf, i, w):
            if not (col_major and w == 0):
                return buf[:, :, bass.ds(i * P, P)]
            v = buf[:, :, CTX:TOK].rearrange("p k (c r) -> p k r c", r=ROWS)
            return v[:, :, bass.ds((i - CCH) * (P // GRID_W), P // GRID_W), :]

        def loops(eng, *stages):
            for stage in stages:
                for i in range(CCH):
                    stage(i, i % 2, 1, True)
            with eng.Fori(CCH // 2, NCH // 2) as pair:
                for stage in stages:
                    for j in range(2):
                        stage(pair * 2 + j, j, 0, False)

        def hsplit(t, w):
            return t[:].rearrange("p k (r c) -> p k r c", c=GRID_W) if (col_major and w == 0) else t[:]

        with nc.Block() as block:
            @block.sync
            def _(sp):
                def body(i, j, w, first):
                    if not first:
                        sp.wait_ge(s_xn, i - 1)
                    sp.dma_start(xt[j][:], src[bass.ds(i * P, P), :]).then_inc(load[j], 16)
                loops(sp, body)

            @block.scalar
            def _(act):
                def stats(i, j, w, first):
                    act.wait_ge(load[j], (i - j) * 8 + 16)
                    if not first:
                        act.wait_ge(s_tr, i - 1)
                    act.activation(xn[j][:], xt[j][:], ACT.Square, accum_out=ss[j][:]).then_inc(s_ss, 1)
                    act.wait_ge(s_ss, i + 1)
                    act.activation(rt[j][:], ss[j][:], ACT.Sqrt, bias=T["eps"][:], scale=1.0 / D).then_inc(s_rt, 1)

                def high(i, j, w, first):
                    act.wait_ge(s_h, i + 1)
                    act.activation(place(hi, i, w), hsplit(h[j], w), ACT.Copy).then_inc(s_hi, 1)
                loops(act, stats, high)

            @block.vector
            def _(dve):
                def scale(i, j, w, first):
                    dve.wait_ge(s_rt, i + 1)
                    dve.reciprocal(rs[j][:], rt[j][:]).then_inc(s_rs, 1)
                    dve.wait_ge(s_rs, i + 1)
                    dve.tensor_scalar(xn[j][:], xt[j][:], rs[j][:], None, ALU.mult).then_inc(s_xn, 1)

                def modulate(i, j, w, first):
                    dve.wait_ge(s_tr, i + 1)
                    if not first:
                        dve.wait_ge(s_lo, i - 1)
                    a = T["coef"][:, layer, 0, w].unsqueeze(2).broadcast_to([P, KT, P])
                    b = T["coef"][:, layer, 1, w].unsqueeze(2).broadcast_to([P, KT, P])
                    dve.tensor_tensor(h[j][:], tp[j][:], a, ALU.mult).then_inc(s_mul, 1)
                    dve.wait_ge(s_mul, i + 1)
                    dve.tensor_tensor(h[j][:], h[j][:], b, ALU.add).then_inc(s_h, 1)
                loops(dve, scale, modulate)

            @block.gpsimd
            def _(pool):
                def low(i, j, w, first):
                    pool.wait_ge(s_hi, i + 1)
                    pool.tensor_tensor(place(lo, i, w), hsplit(h[j], w), place(hi, i, w).bitcast(F32),
                                       ALU.subtract).then_inc(s_lo, 1)
                loops(pool, low)

            @block.tensor
            def _(pe):
                def turn(i, j, w, first):
                    pe.wait_ge(s_xn, i + 1)
                    if not first:
                        pe.wait_ge(s_mul, i - 1)
                    for k in range(KT):
                        t = pe.transpose(tp[j][:, k, :], xn[j][:, k * P:(k + 1) * P], T["ident"][:])
                    t.then_inc(s_tr, 1)
                loops(pe, turn)


def phase_gates(nc, sem, T, io, dram, hi, lo):
    W = 4 * NV
    GW = 2 * NV
    CPB = 8
    with ExitStack() as ctx:
        sb = lambda x, s, d=F32: ctx.enter_context(nc.sbuf_tensor("gate_" + x, s, d))
        w = sb("w", [P, KT, W])
        whi, wlo = sb("whi", [P, KT, W], F32R), sb("wlo", [P, KT, W], F32R)
        tri = sb("tri", [P, 2, P])
        alog, dtb = sb("alog", [P, GW]), sb("dtb", [P, GW])
        x = sb("x", [P, NCH, GW])
        y = sb("y", [P, NCH, GW])
        beta = sb("beta", [P, NCH, GW])
        g = sb("g", [P, NCH, GW])
        cg = sb("cg", [P, NCH, GW])
        el = sb("el", [P, NCH, GW])
        nbeg = sb("nbeg", [P, NCH, GW])
        cgT = sb("cgT", [GW, TOK])
        pack = sb("pack", [P, NCH, NQ, 2, NQTY, 2])
        ab = ctx.enter_context(nc.psum_tensor("gate_ab", [P, 3 * CPB, W], F32))
        cs = ctx.enter_context(nc.psum_tensor("gate_cs", [P, 2, 512], F32))
        tot = ctx.enter_context(nc.psum_tensor("gate_tot", [P, 2, 512], F32))
        tp = ab[0:GW].rearrange("p c n -> p (c n)")
        names = ("load", "split", "prod", "x", "beta", "ea", "ln", "pos", "g", "sums", "cg", "d", "eg", "elg", "el",
                 "nbeg", "abs", "exp", "sp", "turned", "row", "copied", "pack", "stored")
        s = {q: sem("gate_" + q) for q in names}

        def dirs(t, dr):
            return t[:, :, dr * NV:(dr + 1) * NV]

        def bank(t, dr):
            return t[:, dr, 0:NCH * NV].rearrange("p (c h) -> p c h", h=NV)

        with nc.Block() as block:
            @block.sync
            def _(sp):
                sp.dma_start(w[:], io["gdn_w_in"][0].rearrange("(k p) n -> p k n", p=P)[:, :, 6144:6208]).then_inc(s["load"], 16)
                sp.dma_start(tri[:], io["tri"]).then_inc(s["load"], 16)
                sp.dma_start(alog[:], io["gdn_a_log"].partition_broadcast(P)).then_inc(s["load"], 16)
                sp.dma_start(dtb[:], io["gdn_dt_bias"].partition_broadcast(P)).then_inc(s["load"], 16)
                sp.wait_ge(s["row"], (NCH + 3) // 4)
                sp.dma_start(dram["cgrow"], cgT[:]).then_inc(s["stored"], 16)
                sp.wait_ge(s["pack"], 1)
                sp.dma_start(dram["gates"].rearrange("c p n -> p c n"),
                             pack[:].rearrange("p c q d m h -> p c (q d m h)")).then_inc(s["stored"], 16)
                sp.wait_ge(s["stored"], 32)

            @block.gpsimd
            def _(pool):
                pool.wait_ge(s["load"], 64)
                pool.tensor_copy(whi[:], w[:]).then_inc(s["split"], 1)
                pool.wait_ge(s["split"], 1)
                pool.tensor_tensor(wlo[:], w[:], whi[:].bitcast(F32), ALU.subtract).then_inc(s["split"], 1)
                n = 0
                for ready, q, t in (("beta", Q_BETA, beta), ("cg", Q_CG, cg), ("nbeg", Q_NBEG, nbeg),
                                    ("elg", Q_ELG, x), ("el", Q_EL, el)):
                    pool.wait_ge(s[ready], 2 if ready == "cg" else 1)
                    for dr in range(2):
                        pool.tensor_copy(pack[:, :, :, dr, q, :], dirs(t, dr).rearrange("p c (q h) -> p c q h", h=2)
                                         ).then_inc(s["copied"], 1)
                        n += 1
                pool.wait_ge(s["copied"], n)
                pool.memset(pack[:, NCH - 1, :, 0, Q_ELG:Q_EL + 1, :], 0.0).then_inc(s["copied"], 1)
                pool.memset(pack[:, CCH, :, 1, Q_ELG:Q_EL + 1, :], 0.0).then_inc(s["copied"], 1)
                pool.wait_ge(s["copied"], n + 2)
                pool.nop().then_inc(s["pack"], 1)

            @block.tensor
            def _(pe):
                pe.wait_ge(s["split"], 2)
                for c in range(NCH):
                    n = 0
                    for k in range(KT):
                        for l, r in ((hi, whi), (hi, wlo), (lo, whi)):
                            i = pe.matmul(ab[:, c, :], l[:, k, c * P:(c + 1) * P], r[:, k, :],
                                          start=(n == 0), stop=(n == 3 * KT - 1))
                            n += 1
                i.then_inc(s["prod"], 1)
                pe.wait_ge(s["g"], 1)
                for dr in range(2):
                    pe.matmul(bank(cs, dr), tri[:, dr, :], dirs(g, dr), start=True, stop=True)
                    i = pe.matmul(bank(tot, dr), T["ones"][:], dirs(g, dr), start=True, stop=True)
                i.then_inc(s["sums"], 1)
                pe.wait_ge(s["cg"], 2)
                pe.wait_ge(s["beta"], 1)
                for n, c0 in enumerate(range(0, NCH, 4)):
                    if n >= 2:
                        pe.wait_ge(s["row"], n - 1)
                    for c in range(c0, min(c0 + 4, NCH)):
                        i = pe.transpose(tp[:, (n % 2) * 512 + (c - c0) * P:(n % 2) * 512 + (c - c0 + 1) * P],
                                         cg[:, c, :], T["ident"][:])
                    i.then_inc(s["turned"], 1)

            @block.scalar
            def _(act):
                act.wait_ge(s["x"], 1)
                abv = ab[:, 0:NCH].rearrange("p c (d m h) -> p c d m h", d=2, m=2)
                act.activation(beta[:].rearrange("p c (d h) -> p c d h", d=2), abv[:, :, :, 1, :], ACT.Sigmoid).then_inc(s["beta"], 1)
                act.activation(alog[:], alog[:], ACT.Exp).then_inc(s["ea"], 1)
                act.activation(y[:], x[:], ACT.Abs).then_inc(s["abs"], 1)
                act.wait_ge(s["abs"], 1)
                act.activation(y[:], y[:], ACT.Exp, scale=-1.0).then_inc(s["exp"], 1)
                act.wait_ge(s["exp"], 1)
                act.activation(y[:], y[:], ACT.Ln, bias=1.0).then_inc(s["ln"], 1)
                act.wait_ge(s["d"], 2)
                act.activation(y[:], cg[:], ACT.Exp).then_inc(s["eg"], 1)
                act.activation(x[:], x[:], ACT.Exp).then_inc(s["elg"], 1)
                for dr in range(2):
                    i = act.activation(dirs(el, dr), bank(tot, dr), ACT.Exp)
                i.then_inc(s["el"], 1)

            @block.vector
            def _(dve):
                dve.wait_ge(s["prod"], 1)
                dve.wait_ge(s["load"], 64)
                abv = ab[:, 0:NCH].rearrange("p c (d m h) -> p c d m h", d=2, m=2)
                db = dtb[:].rearrange("p (d h) -> p d h", d=2).unsqueeze(1).broadcast_to([P, NCH, 2, NV])
                dve.tensor_tensor(x[:].rearrange("p c (d h) -> p c d h", d=2), abv[:, :, :, 0, :], db, ALU.add).then_inc(s["x"], 1)
                dve.wait_ge(s["x"], 1)
                dve.tensor_scalar(g[:], x[:], 0.0, None, ALU.max).then_inc(s["pos"], 1)
                dve.wait_ge(s["pos"], 1)
                dve.wait_ge(s["ln"], 1)
                dve.wait_ge(s["ea"], 1)
                dve.tensor_tensor(g[:], g[:], y[:], ALU.add).then_inc(s["sp"], 1)
                dve.wait_ge(s["sp"], 1)
                dve.scalar_tensor_tensor(g[:], g[:], -1.0, alog[:].unsqueeze(1).broadcast_to([P, NCH, GW]),
                                         ALU.mult, ALU.mult).then_inc(s["g"], 1)
                dve.wait_ge(s["sums"], 1)
                for dr in range(2):
                    dve.tensor_copy(dirs(cg, dr), bank(cs, dr)).then_inc(s["cg"], 1)
                dve.wait_ge(s["cg"], 2)
                for dr in range(2):
                    dve.tensor_tensor(dirs(x, dr), bank(tot, dr), dirs(cg, dr), ALU.subtract).then_inc(s["d"], 1)
                dve.wait_ge(s["eg"], 1)
                dve.scalar_tensor_tensor(nbeg[:], beta[:], -1.0, y[:], ALU.mult, ALU.mult).then_inc(s["nbeg"], 1)
                for n, c0 in enumerate(range(0, NCH, 4)):
                    m = min(4, NCH - c0) * P
                    dve.wait_ge(s["turned"], n + 1)
                    dve.tensor_copy(cgT[:, c0 * P:c0 * P + m], tp[:, (n % 2) * 512:(n % 2) * 512 + m]).then_inc(s["row"], 1)


PAD_L, PAD_R = 2, 1
RAW = TOK + 2 * (PAD_L + PAD_R)
CONV = RAW - PAD_L - PAD_R
LAT0 = CTX + PAD_L + PAD_R


def known(eng, x):
    return x if isinstance(x, int) else eng.snap(x)


def settle(eng, sem):
    eng.sem_inc(sem, 1)


class Projection:

    def __init__(self, nc, sem, ctx, T, name, w, hi, lo, bases, strides):
        self.ones = T["ones"]
        self.w, self.hi, self.lo, self.bases, self.strides = w, hi, lo, bases, strides
        self.T = len(bases)
        assert self.T % 2 == 0
        sb = lambda x, s, d=F32: ctx.enter_context(nc.sbuf_tensor(name + x, s, d))
        self.w32 = [sb(f"w32_{i}", [P, KT, P]) for i in range(2)]
        self.whi = [sb(f"whi{i}", [P, KT, P], F32R) for i in range(2)]
        self.wlo = [sb(f"wlo{i}", [P, KT, P], F32R) for i in range(2)]
        self.bank = [ctx.enter_context(nc.psum_tensor(name + f"bank{i}", [P, 512], F32)) for i in range(NB)]
        self.s_load = [sem(name + f"w_load{i}") for i in range(2)]
        self.s_whi, self.s_split, self.s_mm, self.s_ev = (sem(name + x) for x in ("whi", "split", "mm", "evacuated"))

    def load(self, sp, h, j, first):
        t = h * self.T + j
        col = known(sp, h * self.strides[j] + self.bases[j])
        if not first:
            sp.wait_ge(self.s_split, t - 1)
        src = self.w.rearrange("(k p) n -> p k n", p=P)[:, :, bass.ds(col, P)]
        sp.dma_start(self.w32[j % 2][:], src).then_inc(self.s_load[j % 2], 16)

    def split(self, pool, h, j, first):
        t = h * self.T + j
        b = j % 2
        pool.wait_ge(self.s_load[b], h * (self.T * 8) + 16 * (j // 2 + 1))
        if not first:
            pool.wait_ge(self.s_mm, t * NB - NB)
        pool.tensor_tensor(self.whi[b][:], self.w32[b][:], self.ones[:].unsqueeze(1).broadcast_to([P, KT, P]),
                           ALU.mult).then_inc(self.s_whi, 1)
        pool.wait_ge(self.s_whi, t + 1)
        pool.tensor_tensor(self.wlo[b][:], self.w32[b][:], self.whi[b][:].bitcast(F32), ALU.subtract
                           ).then_inc(self.s_split, 1)

    def products(self, pe, h, j, blk, first):
        t = h * self.T + j
        b = j % 2
        at, n = BLKS[blk]
        if blk == 0:
            pe.wait_ge(self.s_split, t + 1)
        if not first:
            pe.wait_ge(self.s_ev, t * NB - NB + blk + 1)
        m = 0
        for k in range(KT):
            for l, r in ((self.whi, self.hi), (self.whi, self.lo), (self.wlo, self.hi)):
                i = pe.matmul(self.bank[blk][:, 0:n], l[b][:, k, :], r[:, k, at:at + n],
                              start=(m == 0), stop=(m == 3 * KT - 1))
                m += 1
        i.then_inc(self.s_mm, 1)


def raw_row(raw, blk):
    at, n = BLKS[blk]
    at += PAD_L if blk == 0 else 2 * PAD_L + PAD_R
    return raw[:, at:at + n]


def sequences(row):
    return row[:, 0:CTX], row[:, LAT0:LAT0 + SEQ]


def phase_project_gdn(nc, sem, T, io, dram, hi, lo):
    KINDS = ["q", "k", "v", "v", "z", "z"]
    QKW, VW = NQ * HD, NV * HD
    bases = [0, QKW, 2 * QKW, 2 * QKW + HD, 2 * QKW + VW, 2 * QKW + VW + HD]
    strides = [HD, HD, 2 * HD, 2 * HD, 2 * HD, 2 * HD]
    NT = len(KINDS)
    TRB = 4
    with ExitStack() as ctx:
        sb = lambda x, s, d=F32: ctx.enter_context(nc.sbuf_tensor("pj_" + x, s, d))
        pr = Projection(nc, sem, ctx, T, "pj_", io["gdn_w_in"][0], hi, lo, bases, strides)
        raw = sb("raw", [P, RAW])
        acc = sb("acc", [P, CONV])
        act_row = sb("row", [P, TOK])
        tm = sb("tm", [P, NCH, P])
        conv_w = sb("conv_w", [P, 4, 32])
        zg = sb("zg", [P, 1])
        epsq = sb("epsq", [P, 1])
        aux = [ctx.enter_context(nc.psum_tensor(f"pj_aux{i}", [P, 512], F32)) for i in range(3)]
        names = ("const", "conv0", "conv1", "conv2", "conv", "pads", "silu", "square", "aux", "aux_read", "recip", "norm",
                 "fm_out", "tm_out", "z_out", "fm_turn")
        s = {q: sem("pj_" + q) for q in names}
        AUX = {"q": ["ss"], "k": ["ss", "tr"], "v": ["tr"], "z": []}
        uses = [NB * len(AUX[k]) for k in KINDS]

        def aux_before(h, j, which):
            return h * sum(uses) + sum(uses[:j]) + (NB if which == "tr" and "ss" in AUX[KINDS[j]] else 0)

        def nth(h, j, kinds):
            return h * sum(k in kinds for k in KINDS) + sum(k in kinds for k in KINDS[:j + 1])

        def sweep(eng, stage):
            for j in range(NT):
                stage(0, j, j == 0)
            with eng.Fori(1, NQ) as h:
                for j in range(NT):
                    stage(h, j, False)

        def prev(h, j):
            return (h, j - 1) if j else (h - 1, NT - 1)

        with nc.Block() as block:
            @block.sync
            def _(sp):
                sp.dma_start(conv_w[:], io["gdn_conv"]).then_inc(s["const"], 16)
                sp.dma_start(zg[:], io["gdn_norm_g"]).then_inc(s["const"], 16)

                def store(h, j):
                    kind = KINDS[j]
                    h0 = known(sp, h * 1 + 0)
                    if kind == "z":
                        head = known(sp, h * 2 + (j - 4))
                        sp.wait_ge(s["conv"], h * NT + j + 1)
                        dst = dram["z"].rearrange("c p n t -> p n c t")[:, bass.ds(head, 1)]
                        sp.dma_start(dst.rearrange("p o c t -> p (o c) t"), acc[:, 0:TOK].rearrange("p (c t) -> p c t", t=P)
                                     ).then_inc(s["z_out"], 16)
                        return
                    if kind in "qk":
                        sp.wait_ge(s["norm"], nth(h, j, "qk"))
                        settle(sp, s["fm_turn"])
                        dst = dram["fm"][bass.ds(h0, 1)].rearrange("h c p m t -> p (h c) m t")[:, :, 1 if kind == "q" else 0]
                        sp.dma_start(dst, act_row[:].rearrange("p (c t) -> p c t", t=P)).then_inc(s["fm_out"], 16)
                    if kind in "kv":
                        sp.wait_ge(s["aux_read"], aux_before(h, j, "tr") + NB)
                        dst = dram["tm"][bass.ds(h0, 1)].rearrange("h c p m t -> p (h c) m t")[:, :, j - 1]
                        sp.dma_start(dst, tm[:]).then_inc(s["tm_out"], 16)

                def stage(h, j, first):
                    if first:
                        pr.load(sp, 0, 0, True)
                        pr.load(sp, 0, 1, True)
                    else:
                        if j + 1 < NT:
                            pr.load(sp, h, j + 1, False)
                        else:
                            pr.load(sp, h + 1, 0, False)
                        store(*prev(h, j))
                for j in range(NT):
                    stage(0, j, j == 0)
                with sp.Fori(1, NQ - 1) as h:
                    for j in range(NT):
                        stage(h, j, False)
                for j in range(NT):
                    if j + 1 < NT:
                        pr.load(sp, NQ - 1, j + 1, False)
                    store(*prev(NQ - 1, j))
                store(NQ - 1, NT - 1)
                sp.wait_ge(s["fm_out"], 16 * nth(NQ - 1, NT - 1, "qk"))
                sp.wait_ge(s["tm_out"], 16 * nth(NQ - 1, NT - 1, "kv"))
                sp.wait_ge(s["z_out"], 16 * nth(NQ - 1, NT - 1, "z"))

            @block.gpsimd
            def _(pool):
                def stage(h, j, first):
                    pr.split(pool, h, j, isinstance(h, int) and j < 2)
                sweep(pool, stage)

            @block.tensor
            def _(pe):
                def norms(h, j):
                    pe.wait_ge(s["square"], nth(h, j, "qk"))
                    base = aux_before(h, j, "ss")
                    for b, (at, n) in enumerate(BLKS):
                        if b >= 3:
                            pe.wait_ge(s["aux_read"], base + b - 2)
                        pe.matmul(aux[b % 3][:, 0:n], T["ones"][:], acc[:, at:at + n], start=True, stop=True
                                  ).then_inc(s["aux"], 1)

                def turn(h, j):
                    if KINDS[j] == "k":
                        pe.wait_ge(s["norm"], nth(h, j, "qk"))
                    else:
                        pe.wait_ge(s["silu"], nth(h, j, "qkv"))
                    base = aux_before(h, j, "tr")
                    for b in range(NB):
                        if b >= 3:
                            pe.wait_ge(s["aux_read"], base + b - 2)
                        elif KINDS[j] == "k" and b == 0:
                            pe.wait_ge(s["aux_read"], base)
                        for c in range(TRB * b, min(TRB * b + TRB, NCH)):
                            i = pe.transpose(aux[b % 3][:, (c % TRB) * P:(c % TRB + 1) * P],
                                             act_row[:, c * P:(c + 1) * P], T["ident"][:])
                        i.then_inc(s["aux"], 1)

                def stage(h, j, first):
                    if not first:
                        a = prev(h, j)
                        kind = KINDS[a[1]]
                    for blk in range(NB):
                        pr.products(pe, h, j, blk, first)
                        if blk == 2 and not first and "ss" in AUX[kind]:
                            norms(*a)
                    if not first and "tr" in AUX[kind]:
                        turn(*a)
                sweep(pe, stage)

            @block.scalar
            def _(act):
                def take(h, j, blk, first):
                    act.wait_ge(pr.s_mm, (h * NT + j) * NB + blk + 1)
                    if blk == 0:
                        if first:
                            act.wait_ge(s["pads"], 1)
                        else:
                            act.wait_ge(s["conv"], h * NT + j)
                    act.activation(raw_row(raw, blk), pr.bank[blk][:, 0:BLKS[blk][1]],
                                   ACT.Silu if KINDS[j] == "z" else ACT.Copy).then_inc(pr.s_ev, 1)

                def silu(h, j):
                    act.wait_ge(s["conv"], h * NT + j + 1)
                    if not (isinstance(h, int) and h == 0 and j == 0):
                        b = j - 1 if j else 3
                        hb = h if j else h - 1
                        if KINDS[b] in "qk":
                            act.wait_ge(s["fm_out"], 16 * nth(hb, b, "qk"))
                        if KINDS[b] in "kv":
                            act.wait_ge(s["aux"], aux_before(hb, b, "tr") + NB)
                    for dst, src in zip((act_row[:, 0:CTX], act_row[:, CTX:TOK]), sequences(acc)):
                        i = act.activation(dst, src, ACT.Silu)
                    i.then_inc(s["silu"], 1)
                    if KINDS[j] in "qk":
                        act.wait_ge(s["silu"], nth(h, j, "qkv"))
                        act.activation(acc[:, 0:TOK], act_row[:], ACT.Square).then_inc(s["square"], 1)

                def root(h, j):
                    base = aux_before(h, j, "ss")
                    q = KINDS[j] == "q"
                    for b, (at, n) in enumerate(BLKS):
                        act.wait_ge(s["aux"], base + b + 1)
                        act.activation(acc[:, at:at + n], aux[b % 3][:, 0:n], ACT.Sqrt,
                                       bias=epsq[:] if q else T["eps"][:], scale=float(HD) if q else 1.0
                                       ).then_inc(s["aux_read"], 1)

                def collect(h, j):
                    base = aux_before(h, j, "tr")
                    if not (isinstance(h, int) and h == 0 and j == 1):
                        act.wait_ge(s["tm_out"], 16 * nth(h, j, "kv") - 16)
                    for b in range(NB):
                        n = min(TRB, NCH - TRB * b)
                        act.wait_ge(s["aux"], base + b + 1)
                        act.activation(tm[:, TRB * b:TRB * b + n].rearrange("p c t -> p (c t)"),
                                       aux[b % 3][:, 0:n * P], ACT.Copy).then_inc(s["aux_read"], 1)

                def stage(h, j, first):
                    a = None if first else prev(h, j)
                    kind = KINDS[a[1]] if a else "z"
                    take(h, j, 0, first)
                    take(h, j, 1, first)
                    if kind in "qkv":
                        silu(*a)
                    take(h, j, 2, first)
                    if kind in "qk":
                        root(*a)
                    take(h, j, 3, first)
                    take(h, j, 4, first)
                    if kind in "kv":
                        collect(*a)
                sweep(act, stage)

            @block.vector
            def _(dve):
                dve.memset(raw[:], 0.0).then_inc(s["pads"], 1)
                dve.memset(epsq[:], EPS * HD)
                dve.wait_ge(s["const"], 32)

                def normalise(h, j):
                    dve.wait_ge(s["aux_read"], aux_before(h, j, "ss") + NB)
                    dve.reciprocal(acc[:, 0:TOK], acc[:, 0:TOK]).then_inc(s["recip"], 1)
                    dve.wait_ge(s["recip"], nth(h, j, "qk"))
                    dve.tensor_tensor(act_row[:], act_row[:], acc[:, 0:TOK], ALU.mult).then_inc(s["norm"], 1)

                def conv(h, j, first):
                    t = h * NT + j
                    dve.wait_ge(pr.s_ev, t * NB + NB)
                    if not first:
                        kind = KINDS[prev(h, j)[1]]
                        if kind == "v":
                            dve.wait_ge(s["silu"], nth(*prev(h, j), "qkv"))
                        elif kind == "z":
                            dve.wait_ge(s["z_out"], 16 * nth(*prev(h, j), "z"))
                        else:
                            dve.wait_ge(s["norm"], nth(*prev(h, j), "qk"))
                    if KINDS[j] == "z":
                        for dst, at, n in ((acc[:, 0:CTX], PAD_L, CTX), (acc[:, CTX:TOK], LAT0 + PAD_L, SEQ)):
                            i = dve.tensor_scalar(dst, raw[:, at:at + n], zg[:], None, ALU.mult)
                        i.then_inc(s["conv"], 1)
                        return
                    f = h + {0: 0, 1: NQ}[j] if j < 2 else h * 2 + 2 * NQ + (j - 2)
                    tap = lambda m: conv_w[:, m, bass.ds(f, 1)]
                    dve.tensor_scalar(acc[:], raw[:, 0:CONV], tap(0), None, ALU.mult).then_inc(s["conv0"], 1)
                    n = nth(h, j, "qkv")
                    for m in (1, 2, 3):
                        dve.wait_ge(s[f"conv{m - 1}"], n)
                        dve.scalar_tensor_tensor(acc[:], raw[:, m:m + CONV], tap(m), acc[:], ALU.mult, ALU.add
                                                 ).then_inc(s[f"conv{m}"] if m < 3 else s["conv"], 1)

                def stage(h, j, first):
                    if not first and KINDS[prev(h, j)[1]] in "qk":
                        normalise(*prev(h, j))
                    conv(h, j, first)
                sweep(dve, stage)


def phase_delta_core(nc, sem, T, io, dram):
    NPAIR = NSTEP // 2
    LV = NLEV - 1
    YU = RU = XU = LV + 1

    def chunk(dr, n):
        return n if dr == 0 else (CCH - 1 - n if n < CCH else NCH + CCH - 1 - n)

    with ExitStack() as ctx:
        sb = lambda x, s, d=F32: ctx.enter_context(nc.sbuf_tensor("dc_" + x, s, d))
        four = lambda x, s, d=F32: [[sb(f"{x}{q}{p}", s, d) for p in range(2)] for q in range(2)]
        two = lambda x, s, d=F32: [sb(f"{x}{p}", s, d) for p in range(2)]
        C4 = [P, 2, 2, P]
        incl, strict = sb("incl", [P, 2, P]), sb("strict", [P, 2, P])
        lev, id16 = sb("levels", [P, NLEV, 2, P], F16), sb("id16", [P, 4 * P], F16)
        fm = four("fm", [P, 2, 2, P])
        cgr = four("cgr", C4)
        gi, gr = four("gi", [P, 2, NQTY, 2]), four("gr", [P, 2, NQTY, 2])
        kr = four("kr", [P, 2, P])
        tm = four("tm", [P, 2, 3, P])
        dec, egr, bm, di = two("dec", C4), two("egr", C4), two("bm", C4), two("di", C4)
        L32, Lhi, Llo = two("L32", C4), four("Lhi", C4, F16), four("Llo", C4, F16)
        X0a, X0, X = two("X0a", C4, F16), two("X0", C4, F16), two("X", C4, F16)
        R, Y = two("R", C4, F16), two("Y", C4, F16)
        Rf, qk, qd = four("Rf", C4), four("qk", C4), four("qd", C4)
        vb, xr, vs, vn, ob = two("vb", C4), two("xr", C4), two("vs", C4), two("vn", C4), two("ob", C4)
        S, Sd = two("S", C4), sb("Sd", C4)
        bank = lambda x: ctx.enter_context(nc.psum_tensor("dc_ps" + x, C4, F32))
        bY, bR, bX = [bank(f"Y{p}") for p in range(2)], [bank(f"R{p}") for p in range(2)], [bank(f"X{p}") for p in range(2)]
        bZ0, bZ1 = bank("Z0"), bank("Z1")
        par = lambda x: [sem(f"dc_{x}{p}") for p in range(2)]
        ld_i = [[sem(f"dc_ldi{q}{p}") for p in range(2)] for q in range(2)]
        ld_r = [[sem(f"dc_ldr{q}{p}") for p in range(2)] for q in range(2)]
        pY, eY, pR, eR, pX, eX = (par(x) for x in ("pY", "eY", "pR", "eR", "pX", "eX"))
        pZ0, eZ0, pZ1, eZ1 = (sem("dc_" + x) for x in ("pZ0", "eZ0", "pZ1", "eZ1"))
        s_dd, s_abs, s_dec, s_egr, s_bm, s_di, s_bd, s_qd, s_lhi, s_llo, s_x1a, s_x1, s_free = (
            par(x) for x in ("dd", "abs", "dec", "egr", "bm", "di", "bd", "qd", "lhi", "llo", "x1a", "x1", "free"))
        s_const, s_vb, s_vs, s_Sd, s_S, s_turn = (sem("dc_" + x) for x in ("const", "vb", "vs", "Sd", "S", "turn"))
        s_out = par("out")

        def of_load(j, q):
            return (j - q) * 48 + 96

        flat = lambda t: t[:].rearrange("p d h t -> p (d h t)")
        comb = lambda t, c: t[:, c // 2, c % 2, :]
        tok = lambda g, m: g[:, :, m, :].unsqueeze(3).broadcast_to(C4)
        heads = lambda t: t.unsqueeze(2).broadcast_to(C4)

        def sweep(body):
            def run(eng):
                body(-2, 0, True, False, False)
                body(-1, 1, True, True, False)
                body(0, 0, True, True, True)
                body(1, 1, True, True, True)
                with eng.Fori(1, NPAIR // 2 - 1) as m:
                    for q in range(2):
                        body(m * 2 + q, q, True, True, True)
                body(NPAIR - 2, 0, False, True, True)
                body(NPAIR - 1, 1, False, False, True)
            return run

        def z1(u, use):
            late = max(0, u - (NSTEP - 4)) if isinstance(u, int) else 0
            return u * 3 + 4 + use - late

        def z1_gram(j, p):
            return 2 * j + p + 1 if isinstance(j, int) and j < 2 else z1(j * 2 + (p - 4), 3)

        def wait(eng, sem, value):
            if not (isinstance(value, int) and value == 0):
                eng.wait_ge(sem, value)

        with nc.Block() as block:
            @block.sync
            def _(sp):
                for dst, src in ((incl, "incl"), (strict, "strict"), (lev, "levels"), (id16, "ident16")):
                    sp.dma_start(dst[:], io[src]).then_inc(s_const, 16)

                def step(h, n, hp, first, last):
                    hs = lambda dn: (h, n - dn) if n >= dn else (h - 1, n - dn + NCH)
                    qp = lambda dn: (((n - dn) // 2 + hp * (NCH // 2)) % 2, n % 2)
                    if not (first and n < 4) and not (last and n >= 4):
                        hh, nn = hs(4)
                        q, p = qp(4)
                        row = known(sp, hh * 1 + 0)
                        if not (first and n < 8):
                            sp.wait_ge(s_S, hh * NCH + nn - 4 + 2)
                            settle(sp, s_turn)
                        for dr in range(2):
                            c = chunk(dr, nn)
                            sp.dma_start(kr[q][p][:, dr], dram["fm"][bass.ds(row, 1)][:, c].rearrange("o p m t -> (o p) m t")[:, 0]
                                         ).then_inc(ld_r[q][p], 16)
                            sp.dma_start(tm[q][p][:, dr], dram["tm"][bass.ds(row, 1)][:, c].rearrange("o p m t -> (o p) m t")
                                         ).then_inc(ld_r[q][p], 16)
                            sp.dma_start(gr[q][p][:, dr], gates_of(row, dr, c)).then_inc(ld_r[q][p], 16)
                    if not last:
                        q, p = qp(0)
                        row = known(sp, h * 1 + 0)
                        if not (first and n < 4):
                            sp.wait_ge(s_free[p], h * (NCH // 2) + (n // 2 - 1))
                            settle(sp, s_turn)
                        for dr in range(2):
                            c = chunk(dr, n)
                            sp.dma_start(fm[q][p][:, dr], dram["fm"][bass.ds(row, 1)][:, c].rearrange("o p m t -> (o p) m t")
                                         ).then_inc(ld_i[q][p], 16)
                            sp.dma_start(cgr[q][p][:, dr], cgrow_of(row, dr, c)).then_inc(ld_i[q][p], 16)
                            sp.dma_start(gi[q][p][:, dr], gates_of(row, dr, c)).then_inc(ld_i[q][p], 16)
                    if not (first and n < 6) and not (last and n >= 6):
                        hh, nn = hs(6)
                        row = known(sp, hh * 1 + 0)
                        sp.wait_ge(eZ1, z1(hh * NCH + nn, 2))
                        settle(sp, s_turn)
                        for dr in range(2):
                            dst = dram["o"][dr, chunk(dr, nn)].rearrange("p (q h) t -> p q h t", h=2)[:, bass.ds(row, 1)]
                            sp.dma_start(dst.rearrange("p o h t -> p (o h) t"), ob[n % 2][:, dr]).then_inc(s_out[n % 2], 16)

                def cgrow_of(row, dr, c):
                    v = dram["cgrow"].rearrange("(d q h) t -> d q h t", d=2, h=2)[dr][bass.ds(row, 1)][:, :, c * P:(c + 1) * P]
                    return v.rearrange("o h t -> (o h) t").partition_broadcast(P)

                def gates_of(row, dr, c):
                    v = dram["gates"][c].rearrange("p (q d m h) -> p q d m h", d=2, m=NQTY, h=2)[:, bass.ds(row, 1), dr]
                    return v.rearrange("p o m h -> p (o m) h")

                for n in range(NCH):
                    step(0, n, 0, True, False)
                for n in range(NCH):
                    step(1, n, 1, False, False)
                with sp.Fori(1, NQ // 2) as hh:
                    for hp in range(2):
                        for n in range(NCH):
                            step(hh * 2 + hp, n, hp, False, False)
                for n in range(6):
                    step(NQ, n, 0, False, True)
                for p in range(2):
                    sp.wait_ge(s_out[p], 32 * NPAIR)

            @block.gpsimd
            def _(pool):
                pool.wait_ge(s_const, 64)

                def differences(j, q, p):
                    pool.wait_ge(ld_i[q][p], of_load(j, q))
                    if not (isinstance(j, int) and j == 0):
                        pool.wait_ge(eZ1, z1_gram(j - 1, p))
                    g = gi[q][p]
                    pool.tensor_tensor(dec[p][:], cgr[q][p][:], tok(g, Q_CG), ALU.subtract).then_inc(s_dd[p], 1)
                    pool.tensor_tensor(bm[p][:], heads(strict[:]), tok(g, Q_BETA), ALU.mult).then_inc(s_bm[p], 1)

                def masks(j, p):
                    pool.wait_ge(s_dec[p], j + 1)
                    pool.wait_ge(s_bm[p], j + 1)
                    pool.tensor_tensor(bm[p][:], dec[p][:], bm[p][:], ALU.mult).then_inc(s_bd[p], 1)
                    pool.tensor_tensor(di[p][:], dec[p][:], heads(incl[:]), ALU.mult).then_inc(s_di[p], 1)

                def decayed_q(j, q, p):
                    pool.wait_ge(s_egr[p], j + 1)
                    if not (isinstance(j, int) and j < 2):
                        pool.wait_ge(pZ1, z1(j * 2 + (p - 4), 2))
                    pool.tensor_tensor(qd[q][p][:], heads(fm[q][p][:, :, 1, :]), egr[p][:], ALU.mult).then_inc(s_qd[p], 1)
                    pool.wait_ge(s_qd[p], j + 1)
                    pool.wait_ge(s_bm[p], j + 1)
                    pool.wait_ge(pZ1, z1_gram(j, p))
                    pool.sem_inc(s_free[p], 1)

                def low(j, q, p):
                    pool.wait_ge(s_lhi[p], j + 1)
                    pool.tensor_tensor(Llo[q][p][:], L32[p][:], Lhi[q][p][:], ALU.subtract).then_inc(s_llo[p], 1)

                def beta_v(i, q, p):
                    u = i * 2 + p
                    pool.wait_ge(ld_r[q][p], of_load(i, q))
                    if not (isinstance(i, int) and i == 0):
                        pool.wait_ge(eZ0, 2 * u - 2)
                    pool.tensor_tensor(vb[p][:], tm[q][p][:, :, 1:3, :], tok(gr[q][p], Q_BETA), ALU.mult).then_inc(s_vb, 1)

                def faded_state(i, q, p):
                    u = i * 2 + p
                    pool.wait_ge(s_S, u + 1)
                    pool.tensor_tensor(Sd[:], S[p][:], tok(gr[q][p], Q_EL), ALU.mult).then_inc(s_Sd, 1)

                @sweep
                def run(i, q, make, inv, rec):
                    if make:
                        for p in range(2):
                            differences(i + 2, q, p)
                    if rec:
                        beta_v(i, q, 0)
                        faded_state(i, q, 0)
                    if make:
                        for p in range(2):
                            masks(i + 2, p)
                    if rec:
                        beta_v(i, q, 1)
                        faded_state(i, q, 1)
                    if make:
                        for p in range(2):
                            decayed_q(i + 2, q, p)
                            low(i + 2, q, p)
                run(pool)

            @block.tensor
            def _(pe):
                pe.wait_ge(s_const, 64)

                def gram(j, q, p):
                    pe.wait_ge(ld_i[q][p], of_load(j, q))
                    wait(pe, eZ1, z1_gram(j, p) - 1)
                    for dr in range(2):
                        m = pe.matmul(bZ1[:, dr], fm[q][p][:, dr, 0, :], fm[q][p][:, dr], start=True, stop=True)
                    m.then_inc(pZ1, 1)

                def first(j, p):
                    pe.wait_ge(s_x1[p], j + 1)
                    wait(pe, eX[p], j * XU)
                    for c in range(4):
                        m = pe.matmul(comb(bX[p], c), comb(X0[p], c), id16[:, 0:P], start=True, stop=True)
                    m.then_inc(pX[p], 1)

                def level_y(j, q, l, p):
                    if l == 0:
                        pe.wait_ge(eX[p], j * XU + 1)
                    else:
                        pe.wait_ge(eR[p], j * RU + l)
                    wait(pe, eY[p], j * YU + l)
                    for c in range(4):
                        m = pe.matmul(comb(bY[p], c), comb(Lhi[q][p], c), comb(R[p], c), start=True, stop=True)
                    m.then_inc(pY[p], 1)

                def level_rx(j, l, p):
                    xs = (X0 if l == 0 else X)[p]
                    pe.wait_ge(eY[p], j * YU + l + 1)
                    wait(pe, eR[p], j * RU + l)
                    pe.wait_ge(eX[p], j * XU + 1 + l)
                    pe.matmul(flat(bR[p]), id16[:, 0:P], flat(R[p]), start=True, stop=False)
                    for c in range(4):
                        m = pe.matmul(comb(bR[p], c), comb(xs, c), comb(Y[p], c), start=False, stop=(c == 3))
                    m.then_inc(pR[p], 1)
                    for c in range(4):
                        m = pe.matmul(comb(bX[p], c), comb(Y[p], c), comb(xs, c), start=True, stop=True)
                    m.then_inc(pX[p], 1)

                def newton_e(j, q, p):
                    pe.wait_ge(eR[p], j * RU + LV)
                    pe.wait_ge(eY[p], j * YU + LV)
                    pe.wait_ge(s_llo[p], j + 1)
                    pe.matmul(flat(bY[p]), id16[:, 0:P], flat(R[p]), start=True, stop=False)
                    for part in (Lhi, Llo):
                        for c in range(4):
                            m = pe.matmul(comb(bY[p], c), comb(part[q][p], c), comb(R[p], c), start=False,
                                          stop=(part is Llo and c == 3))
                    m.then_inc(pY[p], 1)

                def newton_r(j, p):
                    pe.wait_ge(eY[p], j * YU + LV + 1)
                    pe.wait_ge(eX[p], j * XU + XU)
                    pe.matmul(flat(bR[p]), id16[:, 0:P], flat(R[p]), start=True, stop=False)
                    for c in range(4):
                        m = pe.matmul(comb(bR[p], c), comb(X[p], c), comb(Y[p], c), start=False, stop=(c == 3))
                    m.then_inc(pR[p], 1)

                def recur(i, q, p, piece):
                    u = i * 2 + p
                    if piece == 0:
                        pe.wait_ge(ld_r[q][p], of_load(i, q))
                        pe.wait_ge(s_S, u + 1)
                        for dr in range(2):
                            m = pe.matmul(bZ0[:, dr], kr[q][p][:, dr], S[p][:, dr], start=True, stop=True)
                        m.then_inc(pZ0, 1)
                    elif piece == 1:
                        pe.wait_ge(eZ0, 2 * u + 2)
                        pe.wait_ge(eZ1, z1(u, 1) - 1)
                        pe.wait_ge(eR[p], (i + 1) * RU)
                        for c in range(4):
                            m = pe.matmul(comb(bZ1, c), comb(Rf[q][p], c), comb(xr[p], c), start=True, stop=True)
                        m.then_inc(pZ1, 1)
                    else:
                        pe.wait_ge(s_vs, u + 1)
                        for dr in range(2):
                            m = pe.matmul(bZ0[:, dr], tm[q][p][:, dr, 0], vs[p][:, dr], start=True, stop=True)
                        m.then_inc(pZ0, 1)
                        pe.wait_ge(eZ1, z1(u, 1))
                        pe.wait_ge(s_qd[p], i + 1)
                        for c in range(4):
                            pe.matmul(comb(bZ1, c), comb(qd[q][p], c), comb(S[p], c), start=True, stop=False)
                            m = pe.matmul(comb(bZ1, c), comb(qk[q][p], c), comb(vn[p], c), start=False, stop=True)
                        m.then_inc(pZ1, 1)

                @sweep
                def run(i, q, make, inv, rec):
                    j, r = i + 1, 1 - q
                    if inv:
                        for p in range(2):
                            first(j, p)
                    for l in range(LV):
                        if inv:
                            for p in range(2):
                                level_y(j, r, l, p)
                        if rec:
                            recur(i, q, l // 3, l % 3)
                        if make and l == 3:
                            gram(i + 2, q, 0)
                        if inv:
                            for p in range(2):
                                level_rx(j, l, p)
                    if make:
                        gram(i + 2, q, 1)
                    if inv:
                        for p in range(2):
                            newton_e(j, r, p)
                        for p in range(2):
                            newton_r(j, p)
                run(pe)

            @block.scalar
            def _(act):
                def decays(j, q, p):
                    act.wait_ge(s_dd[p], j + 1)
                    act.activation(dec[p][:], dec[p][:], ACT.Abs).then_inc(s_abs[p], 1)
                    act.wait_ge(s_abs[p], j + 1)
                    act.activation(dec[p][:], dec[p][:], ACT.Exp, scale=-1.0).then_inc(s_dec[p], 1)
                    wait(act, s_qd[p], j)
                    act.activation(egr[p][:], cgr[q][p][:], ACT.Exp).then_inc(s_egr[p], 1)

                def high(j, q, p):
                    act.wait_ge(eZ1, z1_gram(j, p))
                    if not (isinstance(j, int) and j < 2):
                        act.wait_ge(pY[p], j * YU - YU)
                    act.activation(Lhi[q][p][:], L32[p][:], ACT.Copy).then_inc(s_lhi[p], 1)

                def first(j, p):
                    act.wait_ge(pX[p], j * XU + 1)
                    act.activation(R[p][:], bX[p][:], ACT.Copy).then_inc(eX[p], 1)

                def level(j, l, p):
                    act.wait_ge(pR[p], j * RU + 1 + l)
                    act.wait_ge(pX[p], j * XU + 1 + l)
                    act.activation(R[p][:], bR[p][:], ACT.Copy).then_inc(eR[p], 1)

                def last(j, q, p):
                    act.wait_ge(pR[p], j * RU + RU)
                    if not (isinstance(j, int) and j < 2):
                        act.wait_ge(pZ1, z1(j * 2 + (p - 4), 1))
                    act.activation(Rf[q][p][:], bR[p][:], ACT.Copy).then_inc(eR[p], 1)

                def recur(i, q, p, piece):
                    u = i * 2 + p
                    if piece == 1:
                        act.wait_ge(pZ1, z1(u, 1))
                        act.wait_ge(s_vs, u + 1)
                        act.activation(vn[p][:], bZ1[:], ACT.Copy).then_inc(eZ1, 1)
                    elif piece == 2:
                        act.wait_ge(pZ1, z1(u, 2))
                        if not (isinstance(i, int) and i == 0):
                            act.wait_ge(s_out[p], i * 32)
                        act.activation(ob[p][:], bZ1[:], ACT.Copy).then_inc(eZ1, 1)

                @sweep
                def run(i, q, make, inv, rec):
                    j, r = i + 1, 1 - q
                    if inv:
                        for p in range(2):
                            first(j, p)
                    for l in range(LV):
                        if rec:
                            recur(i, q, l // 3, l % 3)
                        if inv:
                            for p in range(2):
                                level(j, l, p)
                        if make and l < 2:
                            decays(i + 2, q, l)
                        if make and l == 3:
                            high(i + 2, q, 0)
                    if inv:
                        for p in range(2):
                            last(j, r, p)
                    if make:
                        high(i + 2, q, 1)
                run(act)

            @block.vector
            def _(dve):
                dve.memset(S[0][:], 0.0).then_inc(s_S, 1)
                dve.sem_inc(eZ0, 1)
                dve.wait_ge(s_const, 64)

                def scores(j, q, p):
                    dve.wait_ge(pZ1, z1_gram(j, p))
                    dve.wait_ge(s_bd[p], j + 1)
                    if not (isinstance(j, int) and j == 0):
                        dve.wait_ge(s_llo[p], j)
                    dve.tensor_tensor(L32[p][:], heads(bZ1[:, :, 0]), bm[p][:], ALU.mult)
                    dve.wait_ge(s_di[p], j + 1)
                    dve.tensor_tensor(qk[q][p][:], heads(bZ1[:, :, 1]), di[p][:], ALU.mult).then_inc(eZ1, 1)

                def first(j, q, p):
                    dve.wait_ge(s_lhi[p], j + 1)
                    dve.tensor_tensor(X0a[p][:], Lhi[q][p][:], lev_t(0), ALU.mult).then_inc(s_x1a[p], 1)
                    dve.wait_ge(s_x1a[p], j + 1)
                    if not (isinstance(j, int) and j == 0):
                        dve.wait_ge(pX[p], j * XU - (XU - 2))
                    dve.tensor_tensor(X0[p][:], X0a[p][:], id16[:].rearrange("p (d h t) -> p d h t", d=2, h=2), ALU.add
                                      ).then_inc(s_x1[p], 1)

                lev_t = lambda n: lev[:, n, ::-1, :].unsqueeze(2).broadcast_to(C4)
                lev_r = lambda n: heads(lev[:, n])

                def level(j, l, p):
                    dve.wait_ge(pY[p], j * YU + l + 1)
                    dve.wait_ge(pX[p], j * XU + l + 1)
                    dve.tensor_tensor(Y[p][:], bY[p][:], lev_r(l + 1), ALU.mult).then_inc(eY[p], 1)

                def level_x(j, l, p):
                    dve.wait_ge(pX[p], j * XU + 2 + l)
                    dve.tensor_tensor(X[p][:], bX[p][:], (X0 if l == 0 else X)[p][:], ALU.add).then_inc(eX[p], 1)

                def newton(j, p):
                    dve.wait_ge(pY[p], j * YU + YU)
                    dve.wait_ge(pX[p], j * XU + XU)
                    dve.scalar_tensor_tensor(flat(Y[p]), flat(bY[p]), -1.0, id16[:], ALU.mult, ALU.add).then_inc(eY[p], 1)

                def recur(i, q, p, piece):
                    u = i * 2 + p
                    g = gr[q][p]
                    if piece == 0:
                        dve.wait_ge(s_vb, u + 1)
                        dve.wait_ge(pZ0, 2 * u + 1)
                        if not (isinstance(i, int) and i == 0):
                            dve.wait_ge(pZ1, z1(u - 2, 1))
                        for c in range(4):
                            m = dve.scalar_tensor_tensor(comb(xr[p], c), comb(bZ0, c), g[:, c // 2, Q_NBEG, c % 2:c % 2 + 1],
                                                         comb(vb[p], c), ALU.mult, ALU.add)
                        m.then_inc(eZ0, 1)
                    elif piece == 1:
                        dve.wait_ge(pZ1, z1(u, 1))
                        dve.tensor_tensor(vs[p][:], bZ1[:], tok(g, Q_ELG), ALU.mult).then_inc(s_vs, 1)
                    else:
                        dve.wait_ge(pZ0, 2 * u + 2)
                        dve.wait_ge(s_Sd, u + 1)
                        if not (p == 0 and isinstance(i, int) and i == 0):
                            dve.wait_ge(pZ1, z1(u - 1, 2))
                        dve.tensor_tensor(S[1 - p][:], bZ0[:], Sd[:], ALU.add).then_inc(eZ0, 1)
                        dve.wait_ge(eZ0, 2 * u + 3)
                        dve.sem_inc(s_S, 1)

                @sweep
                def run(i, q, make, inv, rec):
                    j, r = i + 1, 1 - q
                    for l in range(LV):
                        if inv:
                            for p in range(2):
                                level(j, l, p)
                        if rec:
                            recur(i, q, l // 3, l % 3)
                        if make and l == 3:
                            scores(i + 2, q, 0)
                        if inv:
                            for p in range(2):
                                level_x(j, l, p)
                        if make and l == 4:
                            first(i + 2, q, 0)
                    if inv:
                        for p in range(2):
                            newton(j, p)
                    if make:
                        scores(i + 2, q, 1)
                        first(i + 2, q, 1)
                run(dve)


def skewed(eng, front, back):
    f = lambda i, j: front(i, j, 1 if isinstance(i, int) and i < CCH else 0, isinstance(i, int) and i < 2)
    b = lambda i, j: back(i, j, 1 if isinstance(i, int) and i < CCH else 0, isinstance(i, int) and i < 2)
    f(0, 0)
    for i in range(1, 4):
        f(i, i % 2)
        b(i - 1, (i - 1) % 2)
    with eng.Fori(2, NCH // 2) as pair:
        f(pair * 2, 0)
        b(pair * 2 - 1, 1)
        f(pair * 2 + 1, 1)
        b(pair * 2, 0)
    b(NCH - 1, (NCH - 1) % 2)


def gate_rows(pe, coef, layer, w, ident, banks, sem_done):
    for k in range(KT):
        m = pe.matmul(banks[k // 4][:, (k % 4) * P:(k % 4 + 1) * P],
                      coef[:, layer, 2, w, k:k + 1].broadcast_to([P, P]), ident[:], start=True, stop=True)
    m.then_inc(sem_done, 1)


def phase_output_gdn(nc, sem, T, io, dram):
    with ExitStack() as ctx:
        sb = lambda x, s, d=F32: ctx.enter_context(nc.sbuf_tensor("og_" + x, s, d))
        W = NV * HD
        whi, wlo = sb("whi", [P, NV, D], F32R), sb("wlo", [P, NV, D], F32R)
        gate = sb("gate", [P, 2, D])
        of, ob, z = sb("of", [P, NV, P]), sb("ob", [P, NV, P]), sb("z", [P, NV, P])
        hi = [sb(f"hi{j}", [P, NV, P], F32R) for j in range(2)]
        lo = [sb(f"lo{j}", [P, NV, P], F32R) for j in range(2)]
        xt = [sb(f"x{j}", [P, D]) for j in range(2)]
        y = sb("y", [P, D])
        ss = sb("ss", [P, NV])
        tp = [ctx.enter_context(nc.psum_tensor(f"og_tp{i}", [P, 512], F32)) for i in range(4)]
        yp = [[ctx.enter_context(nc.psum_tensor(f"og_y{j}{i}", [P, 512], F32)) for i in range(2)] for j in range(2)]
        w32 = [of[:].rearrange("p a b -> p (a b)")[:, 0:D], ob[:].rearrange("p a b -> p (a b)")[:, 0:D]]
        names = ("w_hi", "w_lo", "gate", "gate_read", "load_o", "load_z", "add", "square", "sum", "root", "recip", "scaled",
                 "turned", "oT", "hi", "lo", "y", "gated", "turn")
        s = {q: sem("og_" + q) for q in names}
        w_load = [sem(f"og_w_load{j}") for j in range(2)]
        load_x = [sem(f"og_load_x{j}") for j in range(2)]
        stored = [sem(f"og_stored{j}") for j in range(2)]
        with nc.Block() as block:
            @block.sync
            def _(sp):
                for k in range(NV):
                    if k >= 2:
                        sp.wait_ge(s["w_lo"], k - 1)
                    sp.dma_start(w32[k % 2], io["gdn_w_out"][k * P:(k + 1) * P, :]).then_inc(w_load[k % 2], 16)
                sp.wait_ge(s["w_lo"], NV)

                def front(i, j, w, first):
                    c = known(sp, i * 1 + 0)
                    if not (isinstance(i, int) and i == 0):
                        sp.wait_ge(s["turned"], i)
                        settle(sp, s["turn"])
                    sp.dma_start(of[:], dram["o"][0, bass.ds(c, 1)].rearrange("o p n t -> (o p) n t")).then_inc(s["load_o"], 16)
                    sp.dma_start(ob[:], dram["o"][1, bass.ds(c, 1)].rearrange("o p n t -> (o p) n t")).then_inc(s["load_o"], 16)
                    if not (isinstance(i, int) and i == 0):
                        sp.wait_ge(s["lo"], i)
                        settle(sp, s["turn"])
                    sp.dma_start(z[:], dram["z"][bass.ds(c, 1)].rearrange("o p n t -> (o p) n t")).then_inc(s["load_z"], 16)
                    if not first:
                        sp.wait_ge(stored[j], (i - j) * 8)
                        settle(sp, s["turn"])
                    sp.dma_start(xt[j][:], io["tokens"][bass.ds(c * P, P), :]).then_inc(load_x[j], 16)

                def back(i, j, w, first):
                    c = known(sp, i * 1 + 0)
                    sp.wait_ge(s["gated"], i * 2 + 2)
                    settle(sp, s["turn"])
                    sp.dma_start(dram["tokens1"][bass.ds(c * P, P), :], xt[j][:]).then_inc(stored[j], 16)
                skewed(sp, front, back)
                for j in range(2):
                    sp.wait_ge(stored[j], 8 * NCH)

            @block.gpsimd
            def _(pool):
                for k in range(NV):
                    pool.wait_ge(s["w_hi"], k + 1)
                    pool.tensor_tensor(wlo[:, k, :], w32[k % 2], whi[:, k, :].bitcast(F32), ALU.subtract).then_inc(s["w_lo"], 1)

                def front(i, j, w, first):
                    pool.wait_ge(s["recip"], i + 1)
                    pool.tensor_tensor(of[:], of[:], ss[:].unsqueeze(2).broadcast_to([P, NV, P]), ALU.mult).then_inc(s["scaled"], 1)
                    pool.wait_ge(s["hi"], i + 1)
                    if not first:
                        pool.wait_ge(s["y"], i - 1)
                    pool.tensor_tensor(lo[j][:], z[:], hi[j][:].bitcast(F32), ALU.subtract).then_inc(s["lo"], 1)
                skewed(pool, front, lambda *a: None)

            @block.scalar
            def _(act):
                for k in range(NV):
                    act.wait_ge(w_load[k % 2], 16 * (k // 2 + 1))
                    act.activation(whi[:, k, :], w32[k % 2], ACT.Copy).then_inc(s["w_hi"], 1)

                def front(i, j, w, first):
                    act.wait_ge(s["add"], i + 1)
                    act.activation(ob[:], of[:], ACT.Square).then_inc(s["square"], 1)
                    act.wait_ge(s["sum"], i + 1)
                    act.activation(ss[:], ss[:], ACT.Sqrt, bias=T["eps"][:], scale=1.0 / HD).then_inc(s["root"], 1)
                    act.wait_ge(s["oT"], i + 1)
                    if not first:
                        act.wait_ge(s["y"], i - 1)
                    act.activation(hi[j][:], z[:], ACT.Copy).then_inc(s["hi"], 1)
                skewed(act, front, lambda *a: None)

            @block.tensor
            def _(pe):
                for w in range(2):
                    gate_rows(pe, T["coef"], 0, w, T["ident"], yp[w], s["gate"])
                pe.wait_ge(s["w_lo"], NV)
                pe.wait_ge(s["gate_read"], 2)

                def front(i, j, w, first):
                    pe.wait_ge(s["scaled"], i + 1)
                    if not (isinstance(i, int) and i == 0):
                        pe.wait_ge(s["oT"], i)
                    for n in range(NV):
                        t = pe.transpose(tp[n // 4][:, (n % 4) * P:(n % 4 + 1) * P], of[:, n, :], T["ident"][:])
                    t.then_inc(s["turned"], 1)

                def back(i, j, w, first):
                    pe.wait_ge(s["lo"], i + 1)
                    if not first:
                        pe.wait_ge(s["gated"], i * 2 - 2)
                    for half in range(2):
                        m = 0
                        for l, r in ((hi, whi), (hi, wlo), (lo, whi)):
                            for k in range(NV):
                                t = pe.matmul(yp[j][half][:], l[j][:, k, :], r[:, k, half * 512:(half + 1) * 512],
                                              start=(m == 0), stop=(m == 3 * NV - 1))
                                m += 1
                    t.then_inc(s["y"], 1)
                skewed(pe, front, back)

            @block.vector
            def _(dve):
                for w in range(2):
                    dve.wait_ge(s["gate"], w + 1)
                    for half in range(2):
                        t = dve.tensor_copy(gate[:, w, half * 512:(half + 1) * 512], yp[w][half][:])
                    t.then_inc(s["gate_read"], 1)

                def front(i, j, w, first):
                    dve.wait_ge(s["load_o"], i * 32 + 32)
                    dve.tensor_tensor(of[:], of[:], ob[:], ALU.add).then_inc(s["add"], 1)
                    dve.wait_ge(s["square"], i + 1)
                    dve.reduce_sum(ss[:], ob[:], AX.X).then_inc(s["sum"], 1)
                    dve.wait_ge(s["root"], i + 1)
                    dve.reciprocal(ss[:], ss[:]).then_inc(s["recip"], 1)
                    dve.wait_ge(s["turned"], i + 1)
                    dve.wait_ge(s["load_z"], i * 16 + 16)
                    for b in range(4):
                        v = z[:, 4 * b:4 * b + 4].rearrange("p a t -> p (a t)")
                        t = dve.tensor_tensor(v, tp[b][:], v, ALU.mult)
                    t.then_inc(s["oT"], 1)

                def back(i, j, w, first):
                    dve.wait_ge(s["y"], i + 1)
                    if not (isinstance(i, int) and i == 0):
                        dve.wait_ge(s["gated"], i * 2)
                    for half in range(2):
                        h = slice(half * 512, (half + 1) * 512)
                        t = dve.tensor_tensor(y[:, h], yp[j][half][:], gate[:, w, h], ALU.mult)
                    t.then_inc(s["gated"], 1)
                    dve.wait_ge(s["gated"], i * 2 + 1)
                    dve.wait_ge(load_x[j], (i - j) * 8 + 16)
                    dve.tensor_tensor(xt[j][:], xt[j][:], y[:], ALU.add).then_inc(s["gated"], 1)
                skewed(dve, front, back)


def phase_project_lru(nc, sem, T, io, dram, hi, lo):
    with ExitStack() as ctx:
        sb = lambda x, s, d=F32: ctx.enter_context(nc.sbuf_tensor("pl_" + x, s, d))
        NT = 2
        pr = Projection(nc, sem, ctx, T, "pl_", io["lru_w_in"][0], hi, lo, [0, D], [P, P])
        raw = [sb(f"raw{j}", [P, RAW]) for j in range(2)]
        acc = [sb(f"acc{j}", [P, CONV]) for j in range(2)]
        cw, cb = sb("conv_w", [P, 4, KT]), sb("conv_b", [P, KT])
        names = ("const", "pads", "conv0", "conv1", "conv2", "ready0", "ready1", "turn")
        s = {q: sem("pl_" + q) for q in names}
        stored = [sem(f"pl_stored{j}") for j in range(2)]

        def sweep(eng, stage):
            for j in range(NT):
                stage(0, j, True)
            with eng.Fori(1, KT) as h:
                for j in range(NT):
                    stage(h, j, False)

        with nc.Block() as block:
            @block.sync
            def _(sp):
                sp.dma_start(cw[:], io["lru_conv_w"]).then_inc(s["const"], 16)
                sp.dma_start(cb[:], io["lru_conv_b"]).then_inc(s["const"], 16)
                for j in range(NT):
                    pr.load(sp, 0, j, True)

                def stage(h, j, more):
                    if more:
                        pr.load(sp, h + 1, j, False)
                    row = known(sp, h * 1 + 0)
                    sp.wait_ge(s[f"ready{j}"], h + 1)
                    settle(sp, s["turn"])
                    dst = dram["xc" if j == 0 else "gate1"][bass.ds(row, 1)].rearrange("o p t -> (o p) t")
                    for d, src in zip((dst[:, 0:CTX], dst[:, CTX:TOK]), sequences(acc[j])):
                        sp.dma_start(d, src).then_inc(stored[j], 16)
                for j in range(NT):
                    stage(0, j, True)
                with sp.Fori(1, KT - 1) as h:
                    for j in range(NT):
                        stage(h, j, True)
                for j in range(NT):
                    stage(KT - 1, j, False)
                for j in range(NT):
                    sp.wait_ge(stored[j], 32 * KT)

            @block.gpsimd
            def _(pool):
                sweep(pool, lambda h, j, first: pr.split(pool, h, j, first))

            @block.tensor
            def _(pe):
                def stage(h, j, first):
                    for blk in range(NB):
                        pr.products(pe, h, j, blk, first and j == 0)
                sweep(pe, stage)

            @block.scalar
            def _(act):
                act.wait_ge(s["pads"], 2)

                def stage(h, j, first):
                    for blk in range(NB):
                        act.wait_ge(pr.s_mm, (h * NT + j) * NB + blk + 1)
                        if blk == 0 and not first:
                            act.wait_ge(s[f"ready{j}"], h)
                        act.activation(raw_row(raw[j], blk), pr.bank[blk][:, 0:BLKS[blk][1]],
                                       ACT.Silu if j else ACT.Copy).then_inc(pr.s_ev, 1)
                sweep(act, stage)

            @block.vector
            def _(dve):
                for j in range(NT):
                    dve.memset(raw[j][:], 0.0).then_inc(s["pads"], 1)
                dve.wait_ge(s["const"], 32)

                def stage(h, j, first):
                    dve.wait_ge(pr.s_ev, (h * NT + j) * NB + NB)
                    if not first:
                        dve.wait_ge(stored[j], h * 32)
                    if j:
                        dve.tensor_copy(acc[j][:], raw[j][:, PAD_L:PAD_L + CONV]).then_inc(s["ready1"], 1)
                        return
                    tap = lambda m: cw[:, m, bass.ds(h, 1)]
                    dve.tensor_scalar(acc[j][:], raw[j][:, 0:CONV], tap(0), cb[:, bass.ds(h, 1)], ALU.mult, ALU.add
                                      ).then_inc(s["conv0"], 1)
                    for m in (1, 2, 3):
                        dve.wait_ge(s[f"conv{m - 1}"], h + 1)
                        dve.scalar_tensor_tensor(acc[j][:], raw[j][:, m:m + CONV], tap(m), acc[j][:], ALU.mult, ALU.add
                                                 ).then_inc(s[f"conv{m}"] if m < 3 else s["ready0"], 1)
                sweep(dve, stage)


def phase_scan(nc, sem, T, io, dram):
    S2 = 2
    with ExitStack() as ctx:
        sb = lambda x, s, d=F32: ctx.enter_context(nc.sbuf_tensor("sc_" + x, s, d))
        w32 = sb("w32", [P, 2, 2, 2, 256])
        whi, wlo = sb("whi", [P, 2, 2, 2, 256], F32R), sb("wlo", [P, 2, 2, 2, 256], F32R)
        xc = sb("xc", [P, S2, TOK])
        xhi, xlo = sb("xhi", [P, S2, TOK], F32R), sb("xlo", [P, S2, TOK], F32R)
        gate = sb("gate", [P, S2, SEQ])
        A, I, Tn, V = (sb(x, [P, S2, TOK]) for x in ("A", "I", "T", "V"))
        H = sb("H", [P, S2, SEQ])
        br, bi = sb("br", [P, 2, KT]), sb("bi", [P, 2, KT])
        lam, c8, nc8 = sb("lam", [P, 2, KT]), sb("c8", [P, 2, KT]), sb("nc8", [P, 2, KT])
        tl = sb("tl", [P, 2, KT])
        bank = [ctx.enter_context(nc.psum_tensor(f"sc_b{i}", [P, 512], F32)) for i in range(8)]
        names = ("const", "la", "le", "ln", "lp", "lq", "c8", "nc8", "load", "w_hi", "w_lo", "x_hi", "x_lo", "mm", "ev", "tanh",
                 "a", "sq", "v", "root", "ix", "b", "scan", "ctx_scan", "sum", "mix", "stored", "turn")
        s = {q: sem("sc_" + q) for q in names}
        GR = [(g, t, b) for t in range(S2) for g in range(2) for b in range(NB)]
        NG = len(GR)

        with nc.Block() as block:
            @block.sync
            def _(sp):
                for dst, src in ((br, "lru_b_r"), (bi, "lru_b_i"), (lam, "lru_lambda")):
                    sp.dma_start(dst[:], io[src]).then_inc(s["const"], 16)

                def block_loads(b, first):
                    n = known(sp, b * 1 + 0)
                    if not first:
                        sp.wait_ge(s["ix"], b * 2)
                        sp.wait_ge(s["mix"], b)
                        settle(sp, s["turn"])
                    for d in range(2):
                        for g, w in enumerate(("lru_w_r", "lru_w_i")):
                            src = io[w][d][bass.ds(n, 1)].rearrange("o (k p) n -> p (o k) n", p=P)
                            sp.dma_start(w32[:, d, g], src).then_inc(s["load"], 16)
                    sp.dma_start(xc[:], dram["xc"][bass.ds(n * 2, 2)].rearrange("s p t -> p s t")).then_inc(s["load"], 16)
                    sp.dma_start(gate[:], dram["gate1"][bass.ds(n * 2, 2)].rearrange("s p t -> p s t")[:, :, CTX:TOK]
                                 ).then_inc(s["load"], 16)

                def block_store(b):
                    n = known(sp, b * 1 + 0)
                    sp.wait_ge(s["mix"], b + 1)
                    settle(sp, s["turn"])
                    sp.dma_start(dram["mixed"][bass.ds(n * 2, 2)].rearrange("s p t -> p s t"), Tn[:, :, 0:SEQ]
                                 ).then_inc(s["stored"], 16)
                block_loads(0, True)
                with sp.Fori(0, LB - 1) as b:
                    block_store(b)
                    block_loads(b + 1, False)
                block_store(LB - 1)
                sp.wait_ge(s["stored"], 16 * LB)

            @block.gpsimd
            def _(pool):
                def one(b, first):
                    pool.wait_ge(s["w_hi"], b + 1)
                    pool.tensor_tensor(wlo[:], w32[:], whi[:].bitcast(F32), ALU.subtract).then_inc(s["w_lo"], 1)
                    pool.wait_ge(s["x_hi"], b + 1)
                    pool.tensor_tensor(xlo[:], xc[:], xhi[:].bitcast(F32), ALU.subtract).then_inc(s["x_lo"], 1)
                    for d in range(2):
                        pool.wait_ge(s["ev"], (b * 2 + d + 1) * NG)
                        pool.tensor_tensor(I[:], I[:], xc[:], ALU.mult).then_inc(s["ix"], 1)
                one(0, True)
                with pool.Fori(1, LB) as b:
                    one(b, False)

            @block.tensor
            def _(pe):
                def one(b, first):
                    pe.wait_ge(s["w_lo"], b + 1)
                    pe.wait_ge(s["x_lo"], b + 1)
                    for d in range(2):
                        for n, (g, t, blk) in enumerate(GR):
                            if not (first and d == 0 and n < 4):
                                pe.wait_ge(s["ev"], (b * 2 + d) * NG + n - 3)
                            at, w = BLKS[blk]
                            m = 0
                            for l, r in ((whi, xhi), (whi, xlo), (wlo, xhi)):
                                for k in range(2):
                                    i = pe.matmul(bank[n % 4][:, 0:w], l[:, d, g, k, t * P:(t + 1) * P], r[:, k, at:at + w],
                                                  start=(m == 0), stop=(m == 5))
                                    m += 1
                            i.then_inc(s["mm"], 1)
                one(0, True)
                with pe.Fori(1, LB) as b:
                    one(b, False)

            @block.scalar
            def _(act):
                act.wait_ge(s["const"], 48)
                act.activation(tl[:], lam[:], ACT.Abs).then_inc(s["la"], 1)
                act.wait_ge(s["la"], 1)
                act.activation(tl[:], tl[:], ACT.Exp, scale=-1.0).then_inc(s["le"], 1)
                act.wait_ge(s["le"], 1)
                act.activation(tl[:], tl[:], ACT.Ln, bias=1.0).then_inc(s["ln"], 1)
                act.wait_ge(s["nc8"], 1)

                def one(b, first):
                    act.wait_ge(s["load"], b * 96 + 96)
                    if not first:
                        act.wait_ge(s["mm"], b * (2 * NG))
                    act.activation(whi[:], w32[:], ACT.Copy).then_inc(s["w_hi"], 1)
                    act.activation(xhi[:], xc[:], ACT.Copy).then_inc(s["x_hi"], 1)
                    for d in range(2):
                        u = b * 2 + d
                        if not (first and d == 0):
                            act.wait_ge(s["scan"], u)
                        for n, (g, t, blk) in enumerate(GR):
                            at, w = BLKS[blk]
                            act.wait_ge(s["mm"], u * NG + n + 1)
                            bias = (bi if g else br)[:, d, 2 * b + t:2 * b + t + 1]
                            act.activation((I if g else A)[:, t, at:at + w], bank[n % 4][:, 0:w], ACT.Sigmoid, bias=bias
                                           ).then_inc(s["ev"], 1)
                        act.wait_ge(s["ev"], u * NG + NG)
                        if not (first and d == 0) and d == 0:
                            act.wait_ge(s["stored"], b * 16)
                        for t in range(S2):
                            i = act.activation(Tn[:, t], A[:, t], ACT.Tanh, scale=c8[:, d, 2 * b + t:2 * b + t + 1])
                        i.then_inc(s["tanh"], 1)
                        act.wait_ge(s["tanh"], u + 1)
                        for t in range(S2):
                            i = act.activation(A[:, t], A[:, t], ACT.Exp, scale=nc8[:, d, 2 * b + t:2 * b + t + 1])
                        i.then_inc(s["a"], 1)
                        act.wait_ge(s["a"], u + 1)
                        if u:
                            act.wait_ge(s["sum"], u)
                        act.activation(V[:], A[:], ACT.Square).then_inc(s["sq"], 1)
                        act.wait_ge(s["v"], u + 1)
                        act.activation(V[:], V[:], ACT.Sqrt).then_inc(s["root"], 1)
                for b in range(LB):
                    one(b, b == 0)

            @block.vector
            def _(dve):
                dve.wait_ge(s["ln"], 1)
                dve.tensor_scalar(lam[:], lam[:], -1.0, 0.0, ALU.mult, ALU.max).then_inc(s["lp"], 1)
                dve.wait_ge(s["lp"], 1)
                dve.tensor_tensor(lam[:], lam[:], tl[:], ALU.add).then_inc(s["lq"], 1)
                dve.wait_ge(s["lq"], 1)
                dve.tensor_scalar(c8[:], lam[:], RG_C, None, ALU.mult)
                dve.tensor_scalar(nc8[:], lam[:], -RG_C, None, ALU.mult).then_inc(s["nc8"], 1)

                def one(b, first):
                    for d in range(2):
                        u = b * 2 + d
                        dve.wait_ge(s["sq"], u + 1)
                        dve.scalar_tensor_tensor(V[:], V[:], 1.0, Tn[:], ALU.add, ALU.mult).then_inc(s["v"], 1)
                        dve.wait_ge(s["root"], u + 1)
                        dve.wait_ge(s["ix"], u + 1)
                        dve.tensor_tensor(I[:], V[:], I[:], ALU.mult).then_inc(s["b"], 1)
                        dve.wait_ge(s["b"], u + 1)
                        seqs = (slice(0, CTX), slice(CTX, TOK))
                        turn = lambda v: v if d == 0 else v[:, ::-1]
                        for part in range(2):
                            for t in range(S2):
                                sl = seqs[part]
                                edge = (CTX - 1 if d == 0 else 0)
                                start = 0.0 if part == 0 else V[:, t, edge:edge + 1]
                                i = dve.tensor_tensor_scan(turn(V[:, t, sl]), turn(A[:, t, sl]), turn(I[:, t, sl]), start,
                                                           ALU.mult, ALU.add)
                            if part == 0:
                                i.then_inc(s["ctx_scan"], 1)
                                dve.wait_ge(s["ctx_scan"], u + 1)
                        i.then_inc(s["scan"], 1)
                        dve.wait_ge(s["scan"], u + 1)
                        if d == 0:
                            dve.tensor_copy(H[:], V[:, :, CTX:TOK]).then_inc(s["sum"], 1)
                    dve.wait_ge(s["sum"], b * 2 + 1)
                    dve.tensor_tensor(H[:], H[:], V[:, :, CTX:TOK], ALU.add).then_inc(s["sum"], 1)
                    dve.wait_ge(s["sum"], b * 2 + 2)
                    for t in range(S2):
                        o = Tn[:, t, 0:SEQ].rearrange("p (r c) -> p c r", c=GRID_W)
                        i = dve.tensor_tensor(o, H[:, t].rearrange("p (c r) -> p c r", r=ROWS),
                                              gate[:, t].rearrange("p (c r) -> p c r", r=ROWS), ALU.mult)
                    i.then_inc(s["mix"], 1)
                one(0, True)
                with dve.Fori(1, LB) as b:
                    one(b, False)


def phase_output_lru(nc, sem, T, io, dram, out):
    NTL = SEQ // P
    with ExitStack() as ctx:
        sb = lambda x, s, d=F32: ctx.enter_context(nc.sbuf_tensor("ol_" + x, s, d))
        w32 = sb("w32", [P, KT, D])
        whi, wlo = sb("whi", [P, KT, D], F32R), sb("wlo", [P, KT, D], F32R)
        gate, fg = sb("gate", [P, D]), sb("final_g", [P, D])
        mx = [sb(f"mix{j}", [P, KT, P]) for j in range(2)]
        hi = [sb(f"hi{j}", [P, KT, P], F32R) for j in range(2)]
        lo = [sb(f"lo{j}", [P, KT, P], F32R) for j in range(2)]
        xt = [sb(f"x{j}", [P, D]) for j in range(2)]
        y = [sb(f"y{j}", [P, D]) for j in range(2)]
        ss = [sb(f"ss{j}", [P, 1]) for j in range(2)]
        rs = [sb(f"rs{j}", [P, 1]) for j in range(2)]
        yp = [[ctx.enter_context(nc.psum_tensor(f"ol_y{j}{i}", [P, 512], F32)) for i in range(2)] for j in range(2)]
        gp = [ctx.enter_context(nc.psum_tensor(f"ol_g{i}", [P, 512], F32)) for i in range(2)]
        names = ("const", "w_load", "w_hi", "w_lo", "gate", "gate_read", "hi", "lo", "y", "gated", "res", "sum", "root",
                 "recip", "norm", "final", "turn")
        s = {q: sem("ol_" + q) for q in names}
        load = [sem(f"ol_load{j}") for j in range(2)]
        stored = [sem(f"ol_stored{j}") for j in range(2)]

        def tiles(eng, front, back=lambda *a: None):
            front(0, 0, True)
            front(1, 1, True)
            back(0, 0, True)
            front(2, 0, False)
            back(1, 1, True)
            front(3, 1, False)
            back(2, 0, False)
            with eng.Fori(2, NTL // 2) as pair:
                front(pair * 2, 0, False)
                back(pair * 2 - 1, 1, False)
                front(pair * 2 + 1, 1, False)
                back(pair * 2, 0, False)
            back(NTL - 1, 1, False)

        with nc.Block() as block:
            @block.sync
            def _(sp):
                sp.dma_start(fg[:], io["final_g"].partition_broadcast(P)).then_inc(s["const"], 16)
                sp.dma_start(w32[:], io["lru_w_out"].rearrange("(k p) n -> p k n", p=P)).then_inc(s["w_load"], 16)

                def front(i, j, first):
                    at = known(sp, i * P)
                    if not first:
                        sp.wait_ge(stored[j], (i - j) * 8)
                        settle(sp, s["turn"])
                    sp.dma_start(mx[j][:], dram["mixed"].rearrange("k p t -> p k t")[:, :, bass.ds(at, P)]).then_inc(load[j], 16)
                    sp.dma_start(xt[j][:], dram["tokens1"][bass.ds(at + CTX, P), :]).then_inc(load[j], 16)

                def back(i, j, first):
                    at = known(sp, i * P)
                    sp.wait_ge(s["final"], i + 1)
                    settle(sp, s["turn"])
                    sp.dma_start(out[bass.ds(at, P), :], y[j][:]).then_inc(stored[j], 16)
                tiles(sp, front, back)
                for j in range(2):
                    sp.wait_ge(stored[j], 8 * NTL)

            @block.gpsimd
            def _(pool):
                pool.wait_ge(s["w_hi"], 1)
                pool.tensor_tensor(wlo[:], w32[:], whi[:].bitcast(F32), ALU.subtract).then_inc(s["w_lo"], 1)

                def front(i, j, first):
                    pool.wait_ge(s["hi"], i + 1)
                    if not first:
                        pool.wait_ge(s["y"], i - 1)
                    pool.tensor_tensor(lo[j][:], mx[j][:], hi[j][:].bitcast(F32), ALU.subtract).then_inc(s["lo"], 1)
                tiles(pool, front)

            @block.scalar
            def _(act):
                act.wait_ge(s["w_load"], 16)
                act.activation(whi[:], w32[:], ACT.Copy).then_inc(s["w_hi"], 1)

                def front(i, j, first):
                    act.wait_ge(load[j], (i - j) * 16 + 32)
                    if not first:
                        act.wait_ge(s["y"], i - 1)
                    act.activation(hi[j][:], mx[j][:], ACT.Copy).then_inc(s["hi"], 1)

                def back(i, j, first):
                    act.wait_ge(s["res"], i + 1)
                    act.activation(y[j][:], xt[j][:], ACT.Square, accum_out=ss[j][:]).then_inc(s["sum"], 1)
                    act.wait_ge(s["sum"], i + 1)
                    act.activation(ss[j][:], ss[j][:], ACT.Sqrt, bias=T["eps"][:], scale=1.0 / D).then_inc(s["root"], 1)
                tiles(act, front, back)

            @block.tensor
            def _(pe):
                gate_rows(pe, T["coef"], 1, 0, T["ident"], gp, s["gate"])
                pe.wait_ge(s["w_lo"], 1)

                def back(i, j, first):
                    pe.wait_ge(s["lo"], i + 1)
                    if not first:
                        pe.wait_ge(s["gated"], i - 1)
                    for half in range(2):
                        m = 0
                        for l, r in ((hi, whi), (hi, wlo), (lo, whi)):
                            for k in range(KT):
                                t = pe.matmul(yp[j][half][:], l[j][:, k, :], r[:, k, half * 512:(half + 1) * 512],
                                              start=(m == 0), stop=(m == 3 * KT - 1))
                                m += 1
                    t.then_inc(s["y"], 1)
                tiles(pe, back)

            @block.vector
            def _(dve):
                dve.wait_ge(s["gate"], 1)
                for half in range(2):
                    t = dve.tensor_copy(gate[:, half * 512:(half + 1) * 512], gp[half][:])
                t.then_inc(s["gate_read"], 1)
                dve.wait_ge(s["gate_read"], 1)
                dve.wait_ge(s["const"], 16)

                def front(i, j, first):
                    dve.wait_ge(s["y"], i + 1)
                    if not first:
                        dve.wait_ge(stored[j], (i - j) * 8)
                    for half in range(2):
                        h = slice(half * 512, (half + 1) * 512)
                        t = dve.tensor_tensor(y[j][:, h], yp[j][half][:], gate[:, h], ALU.mult)
                    t.then_inc(s["gated"], 1)
                    dve.wait_ge(s["gated"], i + 1)
                    dve.tensor_tensor(xt[j][:], xt[j][:], y[j][:], ALU.add).then_inc(s["res"], 1)

                def back(i, j, first):
                    dve.wait_ge(s["root"], i + 1)
                    dve.reciprocal(rs[j][:], ss[j][:]).then_inc(s["recip"], 1)
                    dve.wait_ge(s["recip"], i + 1)
                    dve.scalar_tensor_tensor(y[j][:], xt[j][:], rs[j][:], fg[:], ALU.mult, ALU.mult).then_inc(s["final"], 1)
                tiles(dve, front, back)


def build(nc, io, dram, out):
    with ExitStack() as ctx:
        taken = []

        def sem(name):
            taken.append(nc.alloc_semaphore(name))
            return taken[-1]

        def reuse_semaphores():
            nc.clear_and_free_semaphores(taken)
            taken.clear()
            nc.all_engine_barrier()

        T = {
            "ident": ctx.enter_context(nc.sbuf_tensor("ident", [P, P], F32)),
            "ones": ctx.enter_context(nc.sbuf_tensor("ones", [P, P], F32)),
            "coef": ctx.enter_context(nc.sbuf_tensor("coef", [P, 2, 3, 2, KT], F32)),
            "eps": ctx.enter_context(nc.sbuf_tensor("eps_col", [P, 1], F32)),
        }
        phase_modulation(nc, sem, T, io)
        with ExitStack() as c2:
            hi = c2.enter_context(nc.sbuf_tensor("h0_hi", [P, KT, TOK], F32R))
            lo = c2.enter_context(nc.sbuf_tensor("h0_lo", [P, KT, TOK], F32R))
            phase_norm(nc, sem, T, 0, io["tokens"], hi, lo, False)
            phase_gates(nc, sem, T, io, dram, hi, lo)
            phase_project_gdn(nc, sem, T, io, dram, hi, lo)
        phase_delta_core(nc, sem, T, io, dram)
        reuse_semaphores()
        phase_output_gdn(nc, sem, T, io, dram)
        with ExitStack() as c2:
            hi = c2.enter_context(nc.sbuf_tensor("h1_hi", [P, KT, TOK], F32R))
            lo = c2.enter_context(nc.sbuf_tensor("h1_lo", [P, KT, TOK], F32R))
            phase_norm(nc, sem, T, 1, dram["tokens1"], hi, lo, True)
            phase_project_lru(nc, sem, T, io, dram, hi, lo)
        phase_scan(nc, sem, T, io, dram)
        phase_output_lru(nc, sem, T, io, dram, out)


def kernel(**inputs):
    import concourse.bacc as bacc
    from concourse.bass_utils import run_bass_kernel_spmd

    nc = bacc.Bacc("TRN2", target_bir_lowering=False, num_devices=1)
    a = {k: np.asarray(v) for k, v in inputs.items()}
    cols = lambda v: np.ascontiguousarray(np.moveaxis(v.reshape(v.shape[:-1] + (-1, P)), -1, 0))
    i, j = np.arange(P)[:, None], np.arange(P)[None, :]
    lev = np.zeros((P, NLEV, 2, P), np.float16)
    for n in range(NLEV):
        s = 1 << n
        pair = (i // (2 * s) == j // (2 * s))
        up = pair & (i // s % 2 == 0) & (j // s % 2 == 1)
        lev[:, n, 0], lev[:, n, 1] = -1.0 * up, -1.0 * up.T
    arrays = {
        "tokens": np.concatenate([a["ctx"][0], a["x"][0]], 0),
        "cvec": np.ascontiguousarray(np.stack([cols(a["c"][0]), cols(a["c_ctx"])], -1)),
        "mod_w": a["mod_w"], "mod_b": cols(a["mod_b"]), "norm_g": cols(a["norm_g"]),
        "final_g": a["final_g"],
        "gdn_w_in": a["gdn_w_in"], "gdn_conv": cols(a["gdn_conv"][0]),
        "gdn_a_log": a["gdn_a_log"].reshape(-1), "gdn_dt_bias": a["gdn_dt_bias"].reshape(-1),
        "gdn_norm_g": a["gdn_norm_g"].reshape(P, 1), "gdn_w_out": a["gdn_w_out"][0],
        "lru_w_in": a["lru_w_in"], "lru_conv_w": cols(a["lru_conv_w"][0]), "lru_conv_b": cols(a["lru_conv_b"][0]),
        "lru_w_r": a["lru_w_r"][0], "lru_b_r": cols(a["lru_b_r"][0]), "lru_w_i": a["lru_w_i"][0],
        "lru_b_i": cols(a["lru_b_i"][0]), "lru_lambda": cols(a["lru_lambda"][0]), "lru_w_out": a["lru_w_out"][0],
        "ident": np.eye(P, dtype=np.float32), "ident16": np.tile(np.eye(P, dtype=np.float16), (1, 4)),
        "tri": np.stack([i <= j, i >= j], 1).astype(np.float32),
        "incl": np.stack([i <= j, i >= j], 1).astype(np.float32),
        "strict": np.stack([i > j, i < j], 1).astype(np.float32),
        "levels": lev,
    }
    io = {k: nc.dram_tensor("in_" + k, v.shape, mybir.dt.from_np(v.dtype), kind="ExternalInput").ap()
          for k, v in arrays.items()}
    scratch = {
        "gates": (NCH, P, NQ * 2 * NQTY * 2), "cgrow": (2 * NV, TOK),
        "fm": (NQ, NCH, P, 2, P), "tm": (NQ, NCH, P, 3, P), "z": (NCH, P, NV, P),
        "o": (2, NCH, P, NV, P), "tokens1": (TOK, D),
        "xc": (KT, P, TOK), "gate1": (KT, P, TOK), "mixed": (KT, P, SEQ),
    }
    dram = {k: nc.dram_tensor("scratch_" + k, v, F32, kind="Internal").ap() for k, v in scratch.items()}
    out = nc.dram_tensor("out", (SEQ, D), F32, kind="ExternalOutput").ap()
    build(nc, io, dram, out)
    r = run_bass_kernel_spmd(nc, [{"in_" + k: v for k, v in arrays.items()}], core_ids=[0])
    return r.results[0]["out"].reshape(1, SEQ, D)
```

```python
from contextlib import ExitStack

import numpy as np

import concourse.bass as bass
from concourse import mybir

F32 = mybir.dt.float32
F32R = mybir.dt.float32r
F16 = mybir.dt.float16
ACT = mybir.ActivationFunctionType
ALU = mybir.AluOpType
AX = mybir.AxisListType

P = 128
D = 1024
KT = D // P
CTX = 256
SEQ = 2048
GRID_W = 64
ROWS = SEQ // GRID_W
TOK = CTX + SEQ
NCH = TOK // P
CCH = CTX // P
EPS = 1e-6
NQ = 8
NV = 16
HD = 128
BLKS = [(0, CTX)] + [(CTX + 512 * i, 512) for i in range(SEQ // 512)]
NB = len(BLKS)
NLEV = 7
NSTEP = NQ * NCH
RG_C = 8.0
LB = 4
Q_CG, Q_BETA, Q_NBEG, Q_ELG, Q_EL = range(5)
NQTY = 5


def phase_modulation(nc, sem, T, io):
    MT = 3 * KT
    NB512 = 3 * D // 512
    LOADS = 2
    with ExitStack() as ctx:
        sb = lambda n, s, d=F32: ctx.enter_context(nc.sbuf_tensor(n, s, d))
        w = [sb(f"mod_w{l}", [P, KT, 3 * D]) for l in range(2)]
        cvec = sb("cvec", [P, KT, 2])
        sc = sb("silu_c", [P, KT, 2])
        mb = sb("mod_bias", [P, 2, MT])
        ng = sb("norm_g_cols", [P, 2, KT])
        m = sb("mod", [P, 2, MT, 2])
        row = sb("mod_row", [2, 3 * D])
        rowp = [ctx.enter_context(nc.psum_tensor(f"mod_row{n}", [2, 512], F32)) for n in range(NB512)]
        ps = ctx.enter_context(nc.psum_tensor("mod_ps", [P, 2, MT, 2], F32))
        small, silu, rows, copied, prod, vec = (sem(f"mod_{x}") for x in ("small", "silu", "rows", "copied", "prod", "vec"))
        wload = [[sem(f"mod_wload{l}{g}") for g in range(KT // LOADS)] for l in range(2)]
        with nc.Block() as block:
            @block.sync
            def _(sp):
                sp.dma_start(cvec[:], io["cvec"]).then_inc(small, 16)
                sp.dma_start(mb[:], io["mod_b"]).then_inc(small, 16)
                sp.dma_start(ng[:], io["norm_g"]).then_inc(small, 16)
                sp.dma_start(T["ident"][:], io["ident"]).then_inc(small, 16)
                for l in range(2):
                    for k in range(KT):
                        sp.dma_start(w[l][:, k, :], io["mod_w"][l, k * P:(k + 1) * P, :]).then_inc(wload[l][k // LOADS], 16)

            @block.scalar
            def _(act):
                act.wait_ge(small, 64)
                act.activation(sc[:], cvec[:], ACT.Silu).then_inc(silu, 1)

            @block.tensor
            def _(pe):
                pe.wait_ge(silu, 1)
                for l in range(2):
                    for k in range(KT):
                        if k % LOADS == 0:
                            pe.wait_ge(wload[l][k // LOADS], 16 * LOADS)
                        for n in range(NB512):
                            i = pe.matmul(rowp[n][:], sc[:, k, :], w[l][:, k, n * 512:(n + 1) * 512],
                                          start=(k == 0), stop=(k == KT - 1))
                    i.then_inc(rows, 1)
                    pe.wait_ge(copied, l + 1)
                    for mt in range(MT):
                        i = pe.transpose(ps[:, l, mt, :], row[:, mt * P:(mt + 1) * P], T["ident"][0:2, 0:2])
                    i.then_inc(prod, 1)

            @block.vector
            def _(dve):
                coef = T["coef"]
                dve.memset(T["ones"][:], 1.0)
                dve.memset(T["eps"][:], EPS)
                dve.wait_ge(small, 64)
                for l in range(2):
                    dve.wait_ge(rows, l + 1)
                    if l:
                        dve.wait_ge(prod, l)
                    for n in range(NB512):
                        i = dve.tensor_copy(row[:, n * 512:(n + 1) * 512], rowp[n][:])
                    i.then_inc(copied, 1)
                dve.wait_ge(prod, 2)
                dve.tensor_tensor(m[:], ps[:], mb[:].unsqueeze(3).broadcast_to([P, 2, MT, 2]), ALU.add).then_inc(vec, 1)
                dve.wait_ge(vec, 1)
                for l in range(2):
                    mm = m[:, l].rearrange("p (x k) w -> p x w k", x=3)
                    gb = ng[:, l].unsqueeze(1).broadcast_to([P, 2, KT])
                    dve.tensor_copy(coef[:, l, 1], mm[:, 0])
                    dve.tensor_copy(coef[:, l, 2], mm[:, 2])
                    dve.tensor_scalar(coef[:, l, 0], mm[:, 1], 1.0, None, ALU.add).then_inc(vec, 1)
                    dve.wait_ge(vec, 2 + 2 * l)
                    dve.tensor_tensor(coef[:, l, 0], coef[:, l, 0], gb, ALU.mult).then_inc(vec, 1)
                    dve.wait_ge(vec, 3 + 2 * l)


def phase_norm(nc, sem, T, layer, src, hi, lo, col_major):
    n = f"norm{layer}_"
    with ExitStack() as ctx:
        sb = lambda x, s, d=F32: ctx.enter_context(nc.sbuf_tensor(n + x, s, d))
        xt = [sb(f"x{i}", [P, D]) for i in range(2)]
        xn = [sb(f"xn{i}", [P, D]) for i in range(2)]
        h = [sb(f"h{i}", [P, KT, P]) for i in range(2)]
        ss = [sb(f"ss{i}", [P, 1]) for i in range(2)]
        rt = [sb(f"rt{i}", [P, 1]) for i in range(2)]
        rs = [sb(f"rs{i}", [P, 1]) for i in range(2)]
        tp = [ctx.enter_context(nc.psum_tensor(n + f"tp{i}", [P, KT, P], F32)) for i in range(2)]
        load = [sem(n + f"load{i}") for i in range(2)]
        s_ss, s_rt, s_rs, s_xn, s_tr, s_mul, s_h, s_hi, s_lo = (
            sem(n + x) for x in ("ss", "rt", "rs", "xn", "tr", "mul", "h", "hi", "lo"))

        def place(buf, i, w):
            if not (col_major and w == 0):
                return buf[:, :, bass.ds(i * P, P)]
            v = buf[:, :, CTX:TOK].rearrange("p k (c r) -> p k r c", r=ROWS)
            return v[:, :, bass.ds((i - CCH) * (P // GRID_W), P // GRID_W), :]

        def loops(eng, *stages):
            for stage in stages:
                for i in range(CCH):
                    stage(i, i % 2, 1, True)
            with eng.Fori(CCH // 2, NCH // 2) as pair:
                for stage in stages:
                    for j in range(2):
                        stage(pair * 2 + j, j, 0, False)

        def hsplit(t, w):
            return t[:].rearrange("p k (r c) -> p k r c", c=GRID_W) if (col_major and w == 0) else t[:]

        with nc.Block() as block:
            @block.sync
            def _(sp):
                def body(i, j, w, first):
                    if not first:
                        sp.wait_ge(s_xn, i - 1)
                    sp.dma_start(xt[j][:], src[bass.ds(i * P, P), :]).then_inc(load[j], 16)
                loops(sp, body)

            @block.scalar
            def _(act):
                def stats(i, j, w, first):
                    act.wait_ge(load[j], (i - j) * 8 + 16)
                    if not first:
                        act.wait_ge(s_tr, i - 1)
                    act.activation(xn[j][:], xt[j][:], ACT.Square, accum_out=ss[j][:]).then_inc(s_ss, 1)
                    act.wait_ge(s_ss, i + 1)
                    act.activation(rt[j][:], ss[j][:], ACT.Sqrt, bias=T["eps"][:], scale=1.0 / D).then_inc(s_rt, 1)

                def high(i, j, w, first):
                    act.wait_ge(s_h, i + 1)
                    act.activation(place(hi, i, w), hsplit(h[j], w), ACT.Copy).then_inc(s_hi, 1)
                loops(act, stats, high)

            @block.vector
            def _(dve):
                def scale(i, j, w, first):
                    dve.wait_ge(s_rt, i + 1)
                    dve.reciprocal(rs[j][:], rt[j][:]).then_inc(s_rs, 1)
                    dve.wait_ge(s_rs, i + 1)
                    dve.tensor_scalar(xn[j][:], xt[j][:], rs[j][:], None, ALU.mult).then_inc(s_xn, 1)

                def modulate(i, j, w, first):
                    dve.wait_ge(s_tr, i + 1)
                    if not first:
                        dve.wait_ge(s_lo, i - 1)
                    a = T["coef"][:, layer, 0, w].unsqueeze(2).broadcast_to([P, KT, P])
                    b = T["coef"][:, layer, 1, w].unsqueeze(2).broadcast_to([P, KT, P])
                    dve.tensor_tensor(h[j][:], tp[j][:], a, ALU.mult).then_inc(s_mul, 1)
                    dve.wait_ge(s_mul, i + 1)
                    dve.tensor_tensor(h[j][:], h[j][:], b, ALU.add).then_inc(s_h, 1)
                loops(dve, scale, modulate)

            @block.gpsimd
            def _(pool):
                def low(i, j, w, first):
                    pool.wait_ge(s_hi, i + 1)
                    pool.tensor_tensor(place(lo, i, w), hsplit(h[j], w), place(hi, i, w).bitcast(F32),
                                       ALU.subtract).then_inc(s_lo, 1)
                loops(pool, low)

            @block.tensor
            def _(pe):
                def turn(i, j, w, first):
                    pe.wait_ge(s_xn, i + 1)
                    if not first:
                        pe.wait_ge(s_mul, i - 1)
                    for k in range(KT):
                        t = pe.transpose(tp[j][:, k, :], xn[j][:, k * P:(k + 1) * P], T["ident"][:])
                    t.then_inc(s_tr, 1)
                loops(pe, turn)


def phase_gates(nc, sem, T, io, dram, hi, lo):
    W = 4 * NV
    GW = 2 * NV
    CPB = 8
    with ExitStack() as ctx:
        sb = lambda x, s, d=F32: ctx.enter_context(nc.sbuf_tensor("gate_" + x, s, d))
        w = sb("w", [P, KT, W])
        whi, wlo = sb("whi", [P, KT, W], F32R), sb("wlo", [P, KT, W], F32R)
        tri = sb("tri", [P, 2, P])
        alog, dtb = sb("alog", [P, GW]), sb("dtb", [P, GW])
        x = sb("x", [P, NCH, GW])
        y = sb("y", [P, NCH, GW])
        beta = sb("beta", [P, NCH, GW])
        g = sb("g", [P, NCH, GW])
        cg = sb("cg", [P, NCH, GW])
        el = sb("el", [P, NCH, GW])
        nbeg = sb("nbeg", [P, NCH, GW])
        cgT = sb("cgT", [GW, TOK])
        pack = sb("pack", [P, NCH, NQ, 2, NQTY, 2])
        ab = ctx.enter_context(nc.psum_tensor("gate_ab", [P, 3 * CPB, W], F32))
        cs = ctx.enter_context(nc.psum_tensor("gate_cs", [P, 2, 512], F32))
        tot = ctx.enter_context(nc.psum_tensor("gate_tot", [P, 2, 512], F32))
        tp = ab[0:GW].rearrange("p c n -> p (c n)")
        names = ("load", "split", "prod", "x", "beta", "ea", "ln", "pos", "g", "sums", "cg", "d", "eg", "elg", "el",
                 "nbeg", "abs", "exp", "sp", "turned", "row", "copied", "pack", "stored")
        s = {q: sem("gate_" + q) for q in names}

        def dirs(t, dr):
            return t[:, :, dr * NV:(dr + 1) * NV]

        def bank(t, dr):
            return t[:, dr, 0:NCH * NV].rearrange("p (c h) -> p c h", h=NV)

        with nc.Block() as block:
            @block.sync
            def _(sp):
                sp.dma_start(w[:], io["gdn_w_in"][0].rearrange("(k p) n -> p k n", p=P)[:, :, 6144:6208]).then_inc(s["load"], 16)
                sp.dma_start(tri[:], io["tri"]).then_inc(s["load"], 16)
                sp.dma_start(alog[:], io["gdn_a_log"].partition_broadcast(P)).then_inc(s["load"], 16)
                sp.dma_start(dtb[:], io["gdn_dt_bias"].partition_broadcast(P)).then_inc(s["load"], 16)
                sp.wait_ge(s["row"], (NCH + 3) // 4)
                sp.dma_start(dram["cgrow"], cgT[:]).then_inc(s["stored"], 16)
                sp.wait_ge(s["pack"], 1)
                sp.dma_start(dram["gates"].rearrange("c p n -> p c n"),
                             pack[:].rearrange("p c q d m h -> p c (q d m h)")).then_inc(s["stored"], 16)
                sp.wait_ge(s["stored"], 32)

            @block.gpsimd
            def _(pool):
                pool.wait_ge(s["load"], 64)
                pool.tensor_copy(whi[:], w[:]).then_inc(s["split"], 1)
                pool.wait_ge(s["split"], 1)
                pool.tensor_tensor(wlo[:], w[:], whi[:].bitcast(F32), ALU.subtract).then_inc(s["split"], 1)
                n = 0
                for ready, q, t in (("beta", Q_BETA, beta), ("cg", Q_CG, cg), ("nbeg", Q_NBEG, nbeg),
                                    ("elg", Q_ELG, x), ("el", Q_EL, el)):
                    pool.wait_ge(s[ready], 2 if ready == "cg" else 1)
                    for dr in range(2):
                        pool.tensor_copy(pack[:, :, :, dr, q, :], dirs(t, dr).rearrange("p c (q h) -> p c q h", h=2)
                                         ).then_inc(s["copied"], 1)
                        n += 1
                pool.wait_ge(s["copied"], n)
                pool.memset(pack[:, NCH - 1, :, 0, Q_ELG:Q_EL + 1, :], 0.0).then_inc(s["copied"], 1)
                pool.memset(pack[:, CCH, :, 1, Q_ELG:Q_EL + 1, :], 0.0).then_inc(s["copied"], 1)
                pool.wait_ge(s["copied"], n + 2)
                pool.nop().then_inc(s["pack"], 1)

            @block.tensor
            def _(pe):
                pe.wait_ge(s["split"], 2)
                for c in range(NCH):
                    n = 0
                    for k in range(KT):
                        for l, r in ((hi, whi), (hi, wlo), (lo, whi)):
                            i = pe.matmul(ab[:, c, :], l[:, k, c * P:(c + 1) * P], r[:, k, :],
                                          start=(n == 0), stop=(n == 3 * KT - 1))
                            n += 1
                i.then_inc(s["prod"], 1)
                pe.wait_ge(s["g"], 1)
                for dr in range(2):
                    pe.matmul(bank(cs, dr), tri[:, dr, :], dirs(g, dr), start=True, stop=True)
                    i = pe.matmul(bank(tot, dr), T["ones"][:], dirs(g, dr), start=True, stop=True)
                i.then_inc(s["sums"], 1)
                pe.wait_ge(s["cg"], 2)
                pe.wait_ge(s["beta"], 1)
                for n, c0 in enumerate(range(0, NCH, 4)):
                    if n >= 2:
                        pe.wait_ge(s["row"], n - 1)
                    for c in range(c0, min(c0 + 4, NCH)):
                        i = pe.transpose(tp[:, (n % 2) * 512 + (c - c0) * P:(n % 2) * 512 + (c - c0 + 1) * P],
                                         cg[:, c, :], T["ident"][:])
                    i.then_inc(s["turned"], 1)

            @block.scalar
            def _(act):
                act.wait_ge(s["x"], 1)
                abv = ab[:, 0:NCH].rearrange("p c (d m h) -> p c d m h", d=2, m=2)
                act.activation(beta[:].rearrange("p c (d h) -> p c d h", d=2), abv[:, :, :, 1, :], ACT.Sigmoid).then_inc(s["beta"], 1)
                act.activation(alog[:], alog[:], ACT.Exp).then_inc(s["ea"], 1)
                act.activation(y[:], x[:], ACT.Abs).then_inc(s["abs"], 1)
                act.wait_ge(s["abs"], 1)
                act.activation(y[:], y[:], ACT.Exp, scale=-1.0).then_inc(s["exp"], 1)
                act.wait_ge(s["exp"], 1)
                act.activation(y[:], y[:], ACT.Ln, bias=1.0).then_inc(s["ln"], 1)
                act.wait_ge(s["d"], 2)
                act.activation(y[:], cg[:], ACT.Exp).then_inc(s["eg"], 1)
                act.activation(x[:], x[:], ACT.Exp).then_inc(s["elg"], 1)
                for dr in range(2):
                    i = act.activation(dirs(el, dr), bank(tot, dr), ACT.Exp)
                i.then_inc(s["el"], 1)

            @block.vector
            def _(dve):
                dve.wait_ge(s["prod"], 1)
                dve.wait_ge(s["load"], 64)
                abv = ab[:, 0:NCH].rearrange("p c (d m h) -> p c d m h", d=2, m=2)
                db = dtb[:].rearrange("p (d h) -> p d h", d=2).unsqueeze(1).broadcast_to([P, NCH, 2, NV])
                dve.tensor_tensor(x[:].rearrange("p c (d h) -> p c d h", d=2), abv[:, :, :, 0, :], db, ALU.add).then_inc(s["x"], 1)
                dve.wait_ge(s["x"], 1)
                dve.tensor_scalar(g[:], x[:], 0.0, None, ALU.max).then_inc(s["pos"], 1)
                dve.wait_ge(s["pos"], 1)
                dve.wait_ge(s["ln"], 1)
                dve.wait_ge(s["ea"], 1)
                dve.tensor_tensor(g[:], g[:], y[:], ALU.add).then_inc(s["sp"], 1)
                dve.wait_ge(s["sp"], 1)
                dve.scalar_tensor_tensor(g[:], g[:], -1.0, alog[:].unsqueeze(1).broadcast_to([P, NCH, GW]),
                                         ALU.mult, ALU.mult).then_inc(s["g"], 1)
                dve.wait_ge(s["sums"], 1)
                for dr in range(2):
                    dve.tensor_copy(dirs(cg, dr), bank(cs, dr)).then_inc(s["cg"], 1)
                dve.wait_ge(s["cg"], 2)
                for dr in range(2):
                    dve.tensor_tensor(dirs(x, dr), bank(tot, dr), dirs(cg, dr), ALU.subtract).then_inc(s["d"], 1)
                dve.wait_ge(s["eg"], 1)
                dve.scalar_tensor_tensor(nbeg[:], beta[:], -1.0, y[:], ALU.mult, ALU.mult).then_inc(s["nbeg"], 1)
                for n, c0 in enumerate(range(0, NCH, 4)):
                    m = min(4, NCH - c0) * P
                    dve.wait_ge(s["turned"], n + 1)
                    dve.tensor_copy(cgT[:, c0 * P:c0 * P + m], tp[:, (n % 2) * 512:(n % 2) * 512 + m]).then_inc(s["row"], 1)


PAD_L, PAD_R = 2, 1
RAW = TOK + 2 * (PAD_L + PAD_R)
CONV = RAW - PAD_L - PAD_R
LAT0 = CTX + PAD_L + PAD_R


def known(eng, x):
    return x if isinstance(x, int) else eng.snap(x)


def settle(eng, sem):
    eng.sem_inc(sem, 1)


class Projection:

    def __init__(self, nc, sem, ctx, T, name, w, hi, lo, bases, strides):
        self.ones = T["ones"]
        self.w, self.hi, self.lo, self.bases, self.strides = w, hi, lo, bases, strides
        self.T = len(bases)
        assert self.T % 2 == 0
        sb = lambda x, s, d=F32: ctx.enter_context(nc.sbuf_tensor(name + x, s, d))
        self.w32 = [sb(f"w32_{i}", [P, KT, P]) for i in range(2)]
        self.whi = [sb(f"whi{i}", [P, KT, P], F32R) for i in range(2)]
        self.wlo = [sb(f"wlo{i}", [P, KT, P], F32R) for i in range(2)]
        self.bank = [ctx.enter_context(nc.psum_tensor(name + f"bank{i}", [P, 512], F32)) for i in range(NB)]
        self.s_load = [sem(name + f"w_load{i}") for i in range(2)]
        self.s_whi, self.s_split, self.s_mm, self.s_ev = (sem(name + x) for x in ("whi", "split", "mm", "evacuated"))

    def load(self, sp, h, j, first):
        t = h * self.T + j
        col = known(sp, h * self.strides[j] + self.bases[j])
        if not first:
            sp.wait_ge(self.s_split, t - 1)
        src = self.w.rearrange("(k p) n -> p k n", p=P)[:, :, bass.ds(col, P)]
        sp.dma_start(self.w32[j % 2][:], src).then_inc(self.s_load[j % 2], 16)

    def split(self, pool, h, j, first):
        t = h * self.T + j
        b = j % 2
        pool.wait_ge(self.s_load[b], h * (self.T * 8) + 16 * (j // 2 + 1))
        if not first:
            pool.wait_ge(self.s_mm, t * NB - NB)
        pool.tensor_tensor(self.whi[b][:], self.w32[b][:], self.ones[:].unsqueeze(1).broadcast_to([P, KT, P]),
                           ALU.mult).then_inc(self.s_whi, 1)
        pool.wait_ge(self.s_whi, t + 1)
        pool.tensor_tensor(self.wlo[b][:], self.w32[b][:], self.whi[b][:].bitcast(F32), ALU.subtract
                           ).then_inc(self.s_split, 1)

    def products(self, pe, h, j, blk, first):
        t = h * self.T + j
        b = j % 2
        at, n = BLKS[blk]
        if blk == 0:
            pe.wait_ge(self.s_split, t + 1)
        if not first:
            pe.wait_ge(self.s_ev, t * NB - NB + blk + 1)
        m = 0
        for k in range(KT):
            for l, r in ((self.whi, self.hi), (self.whi, self.lo), (self.wlo, self.hi)):
                i = pe.matmul(self.bank[blk][:, 0:n], l[b][:, k, :], r[:, k, at:at + n],
                              start=(m == 0), stop=(m == 3 * KT - 1))
                m += 1
        i.then_inc(self.s_mm, 1)


def raw_row(raw, blk):
    at, n = BLKS[blk]
    at += PAD_L if blk == 0 else 2 * PAD_L + PAD_R
    return raw[:, at:at + n]


def sequences(row):
    return row[:, 0:CTX], row[:, LAT0:LAT0 + SEQ]


def phase_project_gdn(nc, sem, T, io, dram, hi, lo):
    KINDS = ["q", "k", "v", "v", "z", "z"]
    QKW, VW = NQ * HD, NV * HD
    bases = [0, QKW, 2 * QKW, 2 * QKW + HD, 2 * QKW + VW, 2 * QKW + VW + HD]
    strides = [HD, HD, 2 * HD, 2 * HD, 2 * HD, 2 * HD]
    NT = len(KINDS)
    TRB = 4
    with ExitStack() as ctx:
        sb = lambda x, s, d=F32: ctx.enter_context(nc.sbuf_tensor("pj_" + x, s, d))
        pr = Projection(nc, sem, ctx, T, "pj_", io["gdn_w_in"][0], hi, lo, bases, strides)
        raw = sb("raw", [P, RAW])
        acc = sb("acc", [P, CONV])
        act_row = sb("row", [P, TOK])
        tm = sb("tm", [P, NCH, P])
        conv_w = sb("conv_w", [P, 4, 32])
        zg = sb("zg", [P, 1])
        epsq = sb("epsq", [P, 1])
        aux = [ctx.enter_context(nc.psum_tensor(f"pj_aux{i}", [P, 512], F32)) for i in range(3)]
        names = ("const", "conv0", "conv1", "conv2", "conv", "pads", "silu", "square", "aux", "aux_read", "recip", "norm",
                 "fm_out", "tm_out", "z_out", "fm_turn")
        s = {q: sem("pj_" + q) for q in names}
        AUX = {"q": ["ss"], "k": ["ss", "tr"], "v": ["tr"], "z": []}
        uses = [NB * len(AUX[k]) for k in KINDS]

        def aux_before(h, j, which):
            return h * sum(uses) + sum(uses[:j]) + (NB if which == "tr" and "ss" in AUX[KINDS[j]] else 0)

        def nth(h, j, kinds):
            return h * sum(k in kinds for k in KINDS) + sum(k in kinds for k in KINDS[:j + 1])

        def sweep(eng, stage):
            for j in range(NT):
                stage(0, j, j == 0)
            with eng.Fori(1, NQ) as h:
                for j in range(NT):
                    stage(h, j, False)

        def prev(h, j):
            return (h, j - 1) if j else (h - 1, NT - 1)

        with nc.Block() as block:
            @block.sync
            def _(sp):
                sp.dma_start(conv_w[:], io["gdn_conv"]).then_inc(s["const"], 16)
                sp.dma_start(zg[:], io["gdn_norm_g"]).then_inc(s["const"], 16)

                def store(h, j):
                    kind = KINDS[j]
                    h0 = known(sp, h * 1 + 0)
                    if kind == "z":
                        head = known(sp, h * 2 + (j - 4))
                        sp.wait_ge(s["conv"], h * NT + j + 1)
                        dst = dram["z"].rearrange("c p n t -> p n c t")[:, bass.ds(head, 1)]
                        sp.dma_start(dst.rearrange("p o c t -> p (o c) t"), acc[:, 0:TOK].rearrange("p (c t) -> p c t", t=P)
                                     ).then_inc(s["z_out"], 16)
                        return
                    if kind in "qk":
                        sp.wait_ge(s["norm"], nth(h, j, "qk"))
                        settle(sp, s["fm_turn"])
                        dst = dram["fm"][bass.ds(h0, 1)].rearrange("h c p m t -> p (h c) m t")[:, :, 1 if kind == "q" else 0]
                        sp.dma_start(dst, act_row[:].rearrange("p (c t) -> p c t", t=P)).then_inc(s["fm_out"], 16)
                    if kind in "kv":
                        sp.wait_ge(s["aux_read"], aux_before(h, j, "tr") + NB)
                        dst = dram["tm"][bass.ds(h0, 1)].rearrange("h c p m t -> p (h c) m t")[:, :, j - 1]
                        sp.dma_start(dst, tm[:]).then_inc(s["tm_out"], 16)

                def stage(h, j, first):
                    if first:
                        pr.load(sp, 0, 0, True)
                        pr.load(sp, 0, 1, True)
                    else:
                        if j + 1 < NT:
                            pr.load(sp, h, j + 1, False)
                        else:
                            pr.load(sp, h + 1, 0, False)
                        store(*prev(h, j))
                for j in range(NT):
                    stage(0, j, j == 0)
                with sp.Fori(1, NQ - 1) as h:
                    for j in range(NT):
                        stage(h, j, False)
                for j in range(NT):
                    if j + 1 < NT:
                        pr.load(sp, NQ - 1, j + 1, False)
                    store(*prev(NQ - 1, j))
                store(NQ - 1, NT - 1)
                sp.wait_ge(s["fm_out"], 16 * nth(NQ - 1, NT - 1, "qk"))
                sp.wait_ge(s["tm_out"], 16 * nth(NQ - 1, NT - 1, "kv"))
                sp.wait_ge(s["z_out"], 16 * nth(NQ - 1, NT - 1, "z"))

            @block.gpsimd
            def _(pool):
                def stage(h, j, first):
                    pr.split(pool, h, j, isinstance(h, int) and j < 2)
                sweep(pool, stage)

            @block.tensor
            def _(pe):
                def norms(h, j):
                    pe.wait_ge(s["square"], nth(h, j, "qk"))
                    base = aux_before(h, j, "ss")
                    for b, (at, n) in enumerate(BLKS):
                        if b >= 3:
                            pe.wait_ge(s["aux_read"], base + b - 2)
                        pe.matmul(aux[b % 3][:, 0:n], T["ones"][:], acc[:, at:at + n], start=True, stop=True
                                  ).then_inc(s["aux"], 1)

                def turn(h, j):
                    if KINDS[j] == "k":
                        pe.wait_ge(s["norm"], nth(h, j, "qk"))
                    else:
                        pe.wait_ge(s["silu"], nth(h, j, "qkv"))
                    base = aux_before(h, j, "tr")
                    for b in range(NB):
                        if b >= 3:
                            pe.wait_ge(s["aux_read"], base + b - 2)
                        elif KINDS[j] == "k" and b == 0:
                            pe.wait_ge(s["aux_read"], base)
                        for c in range(TRB * b, min(TRB * b + TRB, NCH)):
                            i = pe.transpose(aux[b % 3][:, (c % TRB) * P:(c % TRB + 1) * P],
                                             act_row[:, c * P:(c + 1) * P], T["ident"][:])
                        i.then_inc(s["aux"], 1)

                def stage(h, j, first):
                    if not first:
                        a = prev(h, j)
                        kind = KINDS[a[1]]
                    for blk in range(NB):
                        pr.products(pe, h, j, blk, first)
                        if blk == 2 and not first and "ss" in AUX[kind]:
                            norms(*a)
                        if blk == 1 and j == 3:
                            turn(h, 1)
                    if not first and kind == "v":
                        turn(*a)
                sweep(pe, stage)

            @block.scalar
            def _(act):
                def take(h, j, blk, first):
                    act.wait_ge(pr.s_mm, (h * NT + j) * NB + blk + 1)
                    if blk == 0:
                        if first:
                            act.wait_ge(s["pads"], 1)
                        else:
                            act.wait_ge(s["conv"], h * NT + j)
                    act.activation(raw_row(raw, blk), pr.bank[blk][:, 0:BLKS[blk][1]],
                                   ACT.Silu if KINDS[j] == "z" else ACT.Copy).then_inc(pr.s_ev, 1)

                def silu(h, j):
                    act.wait_ge(s["conv"], h * NT + j + 1)
                    if not (isinstance(h, int) and h == 0 and j == 0):
                        b = j - 1 if j else 3
                        hb = h if j else h - 1
                        if KINDS[b] in "qk":
                            act.wait_ge(s["fm_out"], 16 * nth(hb, b, "qk"))
                        if KINDS[b] in "kv":
                            act.wait_ge(s["aux"], aux_before(hb, b, "tr") + NB)
                    for dst, src in zip((act_row[:, 0:CTX], act_row[:, CTX:TOK]), sequences(acc)):
                        i = act.activation(dst, src, ACT.Silu)
                    i.then_inc(s["silu"], 1)
                    if KINDS[j] in "qk":
                        act.wait_ge(s["silu"], nth(h, j, "qkv"))
                        act.activation(acc[:, 0:TOK], act_row[:], ACT.Square).then_inc(s["square"], 1)

                def root(h, j):
                    base = aux_before(h, j, "ss")
                    q = KINDS[j] == "q"
                    for b, (at, n) in enumerate(BLKS):
                        act.wait_ge(s["aux"], base + b + 1)
                        act.activation(acc[:, at:at + n], aux[b % 3][:, 0:n], ACT.Sqrt,
                                       bias=epsq[:] if q else T["eps"][:], scale=float(HD) if q else 1.0
                                       ).then_inc(s["aux_read"], 1)

                def collect(h, j):
                    base = aux_before(h, j, "tr")
                    if not (isinstance(h, int) and h == 0 and j == 1):
                        act.wait_ge(s["tm_out"], 16 * nth(h, j, "kv") - 16)
                    for b in range(NB):
                        n = min(TRB, NCH - TRB * b)
                        act.wait_ge(s["aux"], base + b + 1)
                        act.activation(tm[:, TRB * b:TRB * b + n].rearrange("p c t -> p (c t)"),
                                       aux[b % 3][:, 0:n * P], ACT.Copy).then_inc(s["aux_read"], 1)

                def stage(h, j, first):
                    a = None if first else prev(h, j)
                    kind = KINDS[a[1]] if a else "z"
                    if j == 3:
                        collect(h, 1)
                    take(h, j, 0, first)
                    take(h, j, 1, first)
                    if kind in "qkv":
                        silu(*a)
                    take(h, j, 2, first)
                    if kind in "qk":
                        root(*a)
                    take(h, j, 3, first)
                    take(h, j, 4, first)
                    if kind == "v":
                        collect(*a)
                sweep(act, stage)

            @block.vector
            def _(dve):
                dve.memset(raw[:], 0.0).then_inc(s["pads"], 1)
                dve.memset(epsq[:], EPS * HD)
                dve.wait_ge(s["const"], 32)

                def normalise(h, j):
                    dve.wait_ge(s["aux_read"], aux_before(h, j, "ss") + NB)
                    dve.reciprocal(acc[:, 0:TOK], acc[:, 0:TOK]).then_inc(s["recip"], 1)
                    dve.wait_ge(s["recip"], nth(h, j, "qk"))
                    dve.tensor_tensor(act_row[:], act_row[:], acc[:, 0:TOK], ALU.mult).then_inc(s["norm"], 1)

                def conv(h, j, first):
                    t = h * NT + j
                    dve.wait_ge(pr.s_ev, t * NB + NB)
                    if not first:
                        kind = KINDS[prev(h, j)[1]]
                        if kind == "v":
                            dve.wait_ge(s["silu"], nth(*prev(h, j), "qkv"))
                        elif kind == "z":
                            dve.wait_ge(s["z_out"], 16 * nth(*prev(h, j), "z"))
                        else:
                            dve.wait_ge(s["norm"], nth(*prev(h, j), "qk"))
                    if KINDS[j] == "z":
                        for dst, at, n in ((acc[:, 0:CTX], PAD_L, CTX), (acc[:, CTX:TOK], LAT0 + PAD_L, SEQ)):
                            i = dve.tensor_scalar(dst, raw[:, at:at + n], zg[:], None, ALU.mult)
                        i.then_inc(s["conv"], 1)
                        return
                    f = h + {0: 0, 1: NQ}[j] if j < 2 else h * 2 + 2 * NQ + (j - 2)
                    tap = lambda m: conv_w[:, m, bass.ds(f, 1)]
                    dve.tensor_scalar(acc[:], raw[:, 0:CONV], tap(0), None, ALU.mult).then_inc(s["conv0"], 1)
                    n = nth(h, j, "qkv")
                    for m in (1, 2, 3):
                        dve.wait_ge(s[f"conv{m - 1}"], n)
                        dve.scalar_tensor_tensor(acc[:], raw[:, m:m + CONV], tap(m), acc[:], ALU.mult, ALU.add
                                                 ).then_inc(s[f"conv{m}"] if m < 3 else s["conv"], 1)

                def stage(h, j, first):
                    if not first and KINDS[prev(h, j)[1]] in "qk":
                        normalise(*prev(h, j))
                    conv(h, j, first)
                sweep(dve, stage)


def phase_delta_core(nc, sem, T, io, dram):
    NPAIR = NSTEP // 2
    LV = NLEV - 1
    YU = RU = XU = LV + 1

    def chunk(dr, n):
        return n if dr == 0 else (CCH - 1 - n if n < CCH else NCH + CCH - 1 - n)

    with ExitStack() as ctx:
        sb = lambda x, s, d=F32: ctx.enter_context(nc.sbuf_tensor("dc_" + x, s, d))
        four = lambda x, s, d=F32: [[sb(f"{x}{q}{p}", s, d) for p in range(2)] for q in range(2)]
        two = lambda x, s, d=F32: [sb(f"{x}{p}", s, d) for p in range(2)]
        C4 = [P, 2, 2, P]
        incl, strict = sb("incl", [P, 2, P]), sb("strict", [P, 2, P])
        lev, id16 = sb("levels", [P, NLEV, 2, P], F16), sb("id16", [P, 4 * P], F16)
        fm = four("fm", [P, 2, 2, P])
        cgr = four("cgr", C4)
        gi, gr = four("gi", [P, 2, NQTY, 2]), four("gr", [P, 2, NQTY, 2])
        kr = four("kr", [P, 2, P])
        tm = four("tm", [P, 2, 3, P])
        dec, egr, bm, di = two("dec", C4), two("egr", C4), two("bm", C4), two("di", C4)
        L32, Lhi, Llo = two("L32", C4), four("Lhi", C4, F16), four("Llo", C4, F16)
        X0a, X0, X = two("X0a", C4, F16), two("X0", C4, F16), two("X", C4, F16)
        R0, R, Y = two("R0", C4, F16), two("R", C4, F16), two("Y", C4, F16)
        qkr = two("qkr", [P, 2, P])
        Rf, qk, qd = four("Rf", C4), four("qk", C4), four("qd", C4)
        vb, xr, vs, vn, ob = two("vb", C4), two("xr", C4), two("vs", C4), two("vn", C4), two("ob", C4)
        S, Sd = two("S", C4), sb("Sd", C4)
        bank = lambda x: ctx.enter_context(nc.psum_tensor("dc_ps" + x, C4, F32))
        bY, bR, bX = [bank(f"Y{p}") for p in range(2)], [bank(f"R{p}") for p in range(2)], [bank(f"X{p}") for p in range(2)]
        bZ0, bZ1 = bank("Z0"), bank("Z1")
        par = lambda x: [sem(f"dc_{x}{p}") for p in range(2)]
        ld_i = [[sem(f"dc_ldi{q}{p}") for p in range(2)] for q in range(2)]
        ld_r = [[sem(f"dc_ldr{q}{p}") for p in range(2)] for q in range(2)]
        pY, eY, pR, eR, pX, eX = (par(x) for x in ("pY", "eY", "pR", "eR", "pX", "eX"))
        pZ0, eZ0, pZ1, eZ1 = (sem("dc_" + x) for x in ("pZ0", "eZ0", "pZ1", "eZ1"))
        s_dd, s_abs, s_dec, s_egr, s_bm, s_qk, s_di, s_raw, s_bd, s_qd, s_lhi, s_llo, s_x1a, s_x1, s_free = (
            par(x) for x in ("dd", "abs", "dec", "egr", "bm", "qk", "di", "raw", "bd", "qd", "lhi", "llo", "x1a", "x1", "free"))
        s_const, s_vb, s_vs, s_Sd, s_S, s_turn = (sem("dc_" + x) for x in ("const", "vb", "vs", "Sd", "S", "turn"))
        s_out = par("out")

        def of_load(j, q):
            return (j - q) * 48 + 96

        flat = lambda t: t[:].rearrange("p d h t -> p (d h t)")
        comb = lambda t, c: t[:, c // 2, c % 2, :]
        tok = lambda g, m: g[:, :, m, :].unsqueeze(3).broadcast_to(C4)
        heads = lambda t: t.unsqueeze(2).broadcast_to(C4)

        def sweep(body):
            def run(eng):
                at = lambda i: body(i, i % 2, i + 3 < NPAIR, -2 <= i < NPAIR - 2, -1 <= i < NPAIR - 1, i >= 0)
                for i in range(-3, 2):
                    at(i)
                with eng.Fori(1, NPAIR // 2 - 2) as m:
                    for q in range(2):
                        body(m * 2 + q, q, True, True, True, True)
                for i in range(NPAIR - 4, NPAIR):
                    at(i)
            return run

        def z1(u, use):
            late = max(0, u + 1 - (NSTEP - 4)) if isinstance(u, int) else 0
            return u * 3 + 4 + use - late

        def z1_gram(j, p):
            return 2 * j + p + 1 if isinstance(j, int) and j < 2 else z1(j * 2 + (p - 4), 1)

        def i_from(i, least):
            return not isinstance(i, int) or i >= least

        def wait(eng, sem, value):
            if not (isinstance(value, int) and value == 0):
                eng.wait_ge(sem, value)

        with nc.Block() as block:
            @block.sync
            def _(sp):
                for dst, src in ((incl, "incl"), (strict, "strict"), (lev, "levels"), (id16, "ident16")):
                    sp.dma_start(dst[:], io[src]).then_inc(s_const, 16)

                def step(h, n, hp, first, last):
                    hs = lambda dn: (h, n - dn) if n >= dn else (h - 1, n - dn + NCH)
                    qp = lambda dn: (((n - dn) // 2 + hp * (NCH // 2)) % 2, n % 2)
                    if not (first and n < 4) and not (last and n >= 4):
                        hh, nn = hs(4)
                        q, p = qp(4)
                        row = known(sp, hh * 1 + 0)
                        if not (first and n < 8):
                            sp.wait_ge(s_S, hh * NCH + nn - 4 + 2)
                            settle(sp, s_turn)
                        for dr in range(2):
                            c = chunk(dr, nn)
                            sp.dma_start(kr[q][p][:, dr], dram["fm"][bass.ds(row, 1)][:, c].rearrange("o p m t -> (o p) m t")[:, 0]
                                         ).then_inc(ld_r[q][p], 16)
                            sp.dma_start(tm[q][p][:, dr], dram["tm"][bass.ds(row, 1)][:, c].rearrange("o p m t -> (o p) m t")
                                         ).then_inc(ld_r[q][p], 16)
                            sp.dma_start(gr[q][p][:, dr], gates_of(row, dr, c)).then_inc(ld_r[q][p], 16)
                    if not last:
                        q, p = qp(0)
                        row = known(sp, h * 1 + 0)
                        if not (first and n < 4):
                            sp.wait_ge(s_free[p], h * (NCH // 2) + (n // 2 - 1))
                            settle(sp, s_turn)
                        for dr in range(2):
                            c = chunk(dr, n)
                            sp.dma_start(fm[q][p][:, dr], dram["fm"][bass.ds(row, 1)][:, c].rearrange("o p m t -> (o p) m t")
                                         ).then_inc(ld_i[q][p], 16)
                            sp.dma_start(cgr[q][p][:, dr], cgrow_of(row, dr, c)).then_inc(ld_i[q][p], 16)
                            sp.dma_start(gi[q][p][:, dr], gates_of(row, dr, c)).then_inc(ld_i[q][p], 16)
                    if not (first and n < 6) and not (last and n >= 6):
                        hh, nn = hs(6)
                        row = known(sp, hh * 1 + 0)
                        sp.wait_ge(eZ1, z1(hh * NCH + nn, 3))
                        settle(sp, s_turn)
                        for dr in range(2):
                            dst = dram["o"][dr, chunk(dr, nn)].rearrange("p (q h) t -> p q h t", h=2)[:, bass.ds(row, 1)]
                            sp.dma_start(dst.rearrange("p o h t -> p (o h) t"), ob[n % 2][:, dr]).then_inc(s_out[n % 2], 16)

                def cgrow_of(row, dr, c):
                    v = dram["cgrow"].rearrange("(d q h) t -> d q h t", d=2, h=2)[dr][bass.ds(row, 1)][:, :, c * P:(c + 1) * P]
                    return v.rearrange("o h t -> (o h) t").partition_broadcast(P)

                def gates_of(row, dr, c):
                    v = dram["gates"][c].rearrange("p (q d m h) -> p q d m h", d=2, m=NQTY, h=2)[:, bass.ds(row, 1), dr]
                    return v.rearrange("p o m h -> p (o m) h")

                for n in range(NCH):
                    step(0, n, 0, True, False)
                for n in range(NCH):
                    step(1, n, 1, False, False)
                with sp.Fori(1, NQ // 2) as hh:
                    for hp in range(2):
                        for n in range(NCH):
                            step(hh * 2 + hp, n, hp, False, False)
                for n in range(6):
                    step(NQ, n, 0, False, True)
                for p in range(2):
                    sp.wait_ge(s_out[p], 32 * NPAIR)

            @block.gpsimd
            def _(pool):
                pool.wait_ge(s_const, 64)

                def differences(j, q, p):
                    pool.wait_ge(ld_i[q][p], of_load(j, q))
                    if not (isinstance(j, int) and j == 0):
                        pool.wait_ge(eZ1, z1_gram(j - 1, p))
                    g = gi[q][p]
                    pool.tensor_tensor(dec[p][:], cgr[q][p][:], tok(g, Q_CG), ALU.subtract).then_inc(s_dd[p], 1)
                    pool.tensor_tensor(bm[p][:], heads(strict[:]), tok(g, Q_BETA), ALU.mult).then_inc(s_bm[p], 1)

                def masks(j, p):
                    pool.wait_ge(s_dec[p], j + 1)
                    pool.wait_ge(s_bm[p], j + 1)
                    pool.tensor_tensor(bm[p][:], dec[p][:], bm[p][:], ALU.mult).then_inc(s_bd[p], 1)
                    pool.tensor_tensor(di[p][:], dec[p][:], heads(incl[:]), ALU.mult).then_inc(s_di[p], 1)

                def attention(j, q, p):
                    pool.wait_ge(eZ1, z1_gram(j, p))
                    if not (isinstance(j, int) and j < 2):
                        pool.wait_ge(pZ1, z1(j * 2 + (p - 4), 3))
                    pool.tensor_tensor(qk[q][p][:], heads(qkr[p][:]), di[p][:], ALU.mult).then_inc(s_qk[p], 1)
                    pool.wait_ge(s_egr[p], j + 1)
                    pool.tensor_tensor(qd[q][p][:], heads(fm[q][p][:, :, 1, :]), egr[p][:], ALU.mult).then_inc(s_qd[p], 1)
                    pool.wait_ge(s_qd[p], j + 1)
                    pool.sem_inc(s_free[p], 1)

                def low(j, q, p):
                    pool.wait_ge(s_lhi[p], j + 1)
                    pool.tensor_tensor(Llo[q][p][:], L32[p][:], Lhi[q][p][:], ALU.subtract).then_inc(s_llo[p], 1)

                def beta_v(i, q, p):
                    u = i * 2 + p
                    pool.wait_ge(ld_r[q][p], of_load(i, q))
                    if not (isinstance(i, int) and i == 0):
                        pool.wait_ge(eZ0, 2 * u - 2)
                    pool.tensor_tensor(vb[p][:], tm[q][p][:, :, 1:3, :], tok(gr[q][p], Q_BETA), ALU.mult).then_inc(s_vb, 1)

                def faded_state(i, q, p):
                    u = i * 2 + p
                    pool.wait_ge(s_S, u + 1)
                    pool.tensor_tensor(Sd[:], S[p][:], tok(gr[q][p], Q_EL), ALU.mult).then_inc(s_Sd, 1)

                @sweep
                def run(i, q, ahead, make, inv, rec):
                    if rec:
                        faded_state(i, q, 0)
                    if make:
                        differences(i + 2, q, 1)
                    if rec:
                        beta_v(i, q, 1)
                    if inv:
                        attention(i + 1, 1 - q, 1)
                    if make:
                        masks(i + 2, 1)
                        low(i + 2, q, 0)
                    if rec:
                        faded_state(i, q, 1)
                    if ahead:
                        differences(i + 3, 1 - q, 0)
                    if inv:
                        beta_v(i + 1, 1 - q, 0)
                    if make:
                        attention(i + 2, q, 0)
                    if ahead:
                        masks(i + 3, 0)
                    if make:
                        low(i + 2, q, 1)
                run(pool)

            @block.tensor
            def _(pe):
                pe.wait_ge(s_const, 64)

                def gram(j, q, p):
                    pe.wait_ge(ld_i[q][p], of_load(j, q))
                    wait(pe, eZ1, z1_gram(j, p) - 1)
                    for dr in range(2):
                        m = pe.matmul(bZ1[:, dr], fm[q][p][:, dr, 0, :], fm[q][p][:, dr], start=True, stop=True)
                    m.then_inc(pZ1, 1)

                def first(j, p):
                    pe.wait_ge(s_x1[p], j + 1)
                    wait(pe, eX[p], j * XU)
                    for c in range(4):
                        m = pe.matmul(comb(bX[p], c), comb(X0[p], c), id16[:, 0:P], start=True, stop=True)
                    m.then_inc(pX[p], 1)

                def level_y(j, q, l, p):
                    if l == 0:
                        pe.wait_ge(eX[p], j * XU + 1)
                    else:
                        pe.wait_ge(eR[p], j * RU + l)
                    wait(pe, eY[p], j * YU + l)
                    for c in range(4):
                        m = pe.matmul(comb(bY[p], c), comb(Lhi[q][p], c), comb((R0 if l == 0 else R)[p], c), start=True, stop=True)
                    m.then_inc(pY[p], 1)

                def level_rx(j, l, p):
                    xs = (X0 if l == 0 else X)[p]
                    pe.wait_ge(eY[p], j * YU + l + 1)
                    wait(pe, eR[p], j * RU + l)
                    pe.wait_ge(eX[p], j * XU + 1 + l)
                    pe.matmul(flat(bR[p]), id16[:, 0:P], flat((R0 if l == 0 else R)[p]), start=True, stop=False)
                    for c in range(4):
                        m = pe.matmul(comb(bR[p], c), comb(xs, c), comb(Y[p], c), start=False, stop=(c == 3))
                    m.then_inc(pR[p], 1)
                    for c in range(4):
                        m = pe.matmul(comb(bX[p], c), comb(Y[p], c), comb(xs, c), start=True, stop=True)
                    m.then_inc(pX[p], 1)

                def newton_e(j, q, p):
                    pe.wait_ge(eR[p], j * RU + LV)
                    pe.wait_ge(eY[p], j * YU + LV)
                    pe.wait_ge(s_llo[p], j + 1)
                    pe.matmul(flat(bY[p]), id16[:, 0:P], flat(R[p]), start=True, stop=False)
                    for part in (Lhi, Llo):
                        for c in range(4):
                            m = pe.matmul(comb(bY[p], c), comb(part[q][p], c), comb(R[p], c), start=False,
                                          stop=(part is Llo and c == 3))
                    m.then_inc(pY[p], 1)

                def newton_r(j, p):
                    pe.wait_ge(eY[p], j * YU + LV + 1)
                    pe.wait_ge(eX[p], j * XU + XU)
                    pe.matmul(flat(bR[p]), id16[:, 0:P], flat(R[p]), start=True, stop=False)
                    for c in range(4):
                        m = pe.matmul(comb(bR[p], c), comb(X[p], c), comb(Y[p], c), start=False, stop=(c == 3))
                    m.then_inc(pR[p], 1)

                def recur(i, q, p, piece):
                    u = i * 2 + p
                    if piece == 0:
                        pe.wait_ge(ld_r[q][p], of_load(i, q))
                        pe.wait_ge(s_S, u + 1)
                        for dr in range(2):
                            m = pe.matmul(bZ0[:, dr], kr[q][p][:, dr], S[p][:, dr], start=True, stop=True)
                        m.then_inc(pZ0, 1)
                    elif piece == 1:
                        pe.wait_ge(eZ0, 2 * u + 2)
                        pe.wait_ge(eZ1, z1(u, 2) - 1)
                        pe.wait_ge(eR[p], (i + 1) * RU)
                        for c in range(4):
                            m = pe.matmul(comb(bZ1, c), comb(Rf[q][p], c), comb(xr[p], c), start=True, stop=True)
                        m.then_inc(pZ1, 1)
                    else:
                        pe.wait_ge(s_vs, u + 1)
                        for dr in range(2):
                            m = pe.matmul(bZ0[:, dr], tm[q][p][:, dr, 0], vs[p][:, dr], start=True, stop=True)
                        m.then_inc(pZ0, 1)

                def outputs(i, q, p, dr):
                    if dr == 0:
                        pe.wait_ge(eZ1, z1(i * 2 + p, 2))
                        pe.wait_ge(s_qk[p], i + 1)
                        pe.wait_ge(s_qd[p], i + 1)
                    for c in (2 * dr, 2 * dr + 1):
                        pe.matmul(comb(bZ1, c), comb(qd[q][p], c), comb(S[p], c), start=True, stop=False)
                        m = pe.matmul(comb(bZ1, c), comb(qk[q][p], c), comb(vn[p], c), start=False, stop=True)
                    if dr:
                        m.then_inc(pZ1, 1)

                @sweep
                def run(i, q, ahead, make, inv, rec):
                    j, r = i + 1, 1 - q
                    for l in range(LV):
                        if inv:
                            for p in range(2):
                                level_y(j, r, l, p)
                        if rec:
                            recur(i, q, l // 3, l % 3)
                        if l == 0 and i_from(i, 1):
                            outputs(i - 1, 1 - q, 1, 1)
                        if rec and l == 3:
                            outputs(i, q, 0, 1)
                        if inv:
                            for p in range(2):
                                level_rx(j, l, p)
                        if rec and l == 2:
                            outputs(i, q, 0, 0)
                        if make and l % 3 == 0:
                            gram(i + 2, q, l // 3)
                    if inv:
                        for p in range(2):
                            newton_e(j, r, p)
                    if make:
                        for p in range(2):
                            first(i + 2, p)
                    if rec:
                        outputs(i, q, 1, 0)
                    if inv:
                        for p in range(2):
                            newton_r(j, p)
                    if not inv and rec:
                        outputs(i, q, 1, 1)
                run(pe)

            @block.scalar
            def _(act):
                def decays(j, q, p):
                    act.wait_ge(s_dd[p], j + 1)
                    act.activation(dec[p][:], dec[p][:], ACT.Abs).then_inc(s_abs[p], 1)
                    act.wait_ge(s_abs[p], j + 1)
                    act.activation(dec[p][:], dec[p][:], ACT.Exp, scale=-1.0).then_inc(s_dec[p], 1)

                def growth(j, q, p):
                    wait(act, s_qd[p], j)
                    act.activation(egr[p][:], cgr[q][p][:], ACT.Exp).then_inc(s_egr[p], 1)

                def raw(j, p):
                    act.wait_ge(pZ1, z1_gram(j, p))
                    wait(act, s_qk[p], j)
                    act.activation(qkr[p][:], bZ1[:, :, 1], ACT.Copy).then_inc(s_raw[p], 1)

                def high(j, q, p):
                    act.wait_ge(eZ1, z1_gram(j, p))
                    if not (isinstance(j, int) and j < 2):
                        act.wait_ge(pY[p], j * YU - YU)
                    act.activation(Lhi[q][p][:], L32[p][:], ACT.Copy).then_inc(s_lhi[p], 1)

                def first(j, p):
                    act.wait_ge(pX[p], j * XU + 1)
                    act.activation(R0[p][:], bX[p][:], ACT.Copy).then_inc(eX[p], 1)

                def level(j, l, p):
                    act.wait_ge(pR[p], j * RU + 1 + l)
                    act.activation(R[p][:], bR[p][:], ACT.Copy).then_inc(eR[p], 1)

                def last(j, q, p):
                    act.wait_ge(pR[p], j * RU + RU)
                    if not (isinstance(j, int) and j < 2):
                        act.wait_ge(pZ1, z1(j * 2 + (p - 4), 2))
                    act.activation(Rf[q][p][:], bR[p][:], ACT.Copy).then_inc(eR[p], 1)

                def recur(i, q, p, piece):
                    u = i * 2 + p
                    if piece == 1:
                        act.wait_ge(pZ1, z1(u, 2))
                        act.wait_ge(s_vs, u + 1)
                        act.activation(vn[p][:], bZ1[:], ACT.Copy).then_inc(eZ1, 1)

                def outputs(i, p):
                    act.wait_ge(pZ1, z1(i * 2 + p, 3))
                    if not (isinstance(i, int) and i == 0):
                        act.wait_ge(s_out[p], i * 32)
                    act.activation(ob[p][:], bZ1[:], ACT.Copy).then_inc(eZ1, 1)

                @sweep
                def run(i, q, ahead, make, inv, rec):
                    j, r = i + 1, 1 - q
                    for l in range(LV):
                        if rec:
                            recur(i, q, l // 3, l % 3)
                        if l == 0 and i_from(i, 1):
                            outputs(i - 1, 1)
                        if rec and l == 3:
                            outputs(i, 0)
                        if inv:
                            for p in range(2):
                                level(j, l, p)
                        if make and l % 3 == 0:
                            raw(i + 2, l // 3)
                            high(i + 2, q, l // 3)
                        if make and l == 1:
                            decays(i + 2, q, 1)
                        if make and l == 2:
                            growth(i + 2, q, 0)
                        if ahead and l == 4:
                            decays(i + 3, 1 - q, 0)
                        if make and l == 5:
                            growth(i + 2, q, 1)
                    if make:
                        for p in range(2):
                            first(i + 2, p)
                    if inv:
                        for p in range(2):
                            last(j, r, p)
                    if not inv and rec:
                        outputs(i, 1)
                run(act)

            @block.vector
            def _(dve):
                dve.memset(S[0][:], 0.0).then_inc(s_S, 1)
                dve.sem_inc(eZ0, 1)
                dve.wait_ge(s_const, 64)

                def scores(j, q, p):
                    dve.wait_ge(pZ1, z1_gram(j, p))
                    dve.wait_ge(s_bd[p], j + 1)
                    if not (isinstance(j, int) and j == 0):
                        dve.wait_ge(s_llo[p], j)
                    dve.wait_ge(s_raw[p], j + 1)
                    dve.tensor_tensor(L32[p][:], heads(bZ1[:, :, 0]), bm[p][:], ALU.mult).then_inc(eZ1, 1)

                def first(j, q, p):
                    dve.wait_ge(s_lhi[p], j + 1)
                    dve.tensor_tensor(X0a[p][:], Lhi[q][p][:], lev_t(0), ALU.mult).then_inc(s_x1a[p], 1)
                    dve.wait_ge(s_x1a[p], j + 1)
                    if not (isinstance(j, int) and j == 0):
                        dve.wait_ge(pX[p], j * XU - (XU - 2))
                    dve.tensor_tensor(X0[p][:], X0a[p][:], id16[:].rearrange("p (d h t) -> p d h t", d=2, h=2), ALU.add
                                      ).then_inc(s_x1[p], 1)

                lev_t = lambda n: lev[:, n, ::-1, :].unsqueeze(2).broadcast_to(C4)
                lev_r = lambda n: heads(lev[:, n])

                def level(j, l, p):
                    dve.wait_ge(pY[p], j * YU + l + 1)
                    dve.wait_ge(pX[p], j * XU + l + 1)
                    dve.tensor_tensor(Y[p][:], bY[p][:], lev_r(l + 1), ALU.mult).then_inc(eY[p], 1)

                def level_x(j, l, p):
                    dve.wait_ge(pX[p], j * XU + 2 + l)
                    dve.tensor_tensor(X[p][:], bX[p][:], (X0 if l == 0 else X)[p][:], ALU.add).then_inc(eX[p], 1)

                def newton(j, p):
                    dve.wait_ge(pY[p], j * YU + YU)
                    dve.wait_ge(pX[p], j * XU + XU)
                    dve.scalar_tensor_tensor(flat(Y[p]), flat(bY[p]), -1.0, id16[:], ALU.mult, ALU.add).then_inc(eY[p], 1)

                def recur(i, q, p, piece):
                    u = i * 2 + p
                    g = gr[q][p]
                    if piece == 0:
                        dve.wait_ge(s_vb, u + 1)
                        dve.wait_ge(pZ0, 2 * u + 1)
                        if not (isinstance(i, int) and i == 0):
                            dve.wait_ge(pZ1, z1(u - 2, 2))
                        for c in range(4):
                            m = dve.scalar_tensor_tensor(comb(xr[p], c), comb(bZ0, c), g[:, c // 2, Q_NBEG, c % 2:c % 2 + 1],
                                                         comb(vb[p], c), ALU.mult, ALU.add)
                        m.then_inc(eZ0, 1)
                    elif piece == 1:
                        dve.wait_ge(pZ1, z1(u, 2))
                        dve.tensor_tensor(vs[p][:], bZ1[:], tok(g, Q_ELG), ALU.mult).then_inc(s_vs, 1)
                    else:
                        dve.wait_ge(pZ0, 2 * u + 2)
                        dve.wait_ge(s_Sd, u + 1)
                        if not (p == 0 and isinstance(i, int) and i == 0):
                            dve.wait_ge(pZ1, z1(u - 1, 3))
                        dve.tensor_tensor(S[1 - p][:], bZ0[:], Sd[:], ALU.add).then_inc(eZ0, 1)
                        dve.wait_ge(eZ0, 2 * u + 3)
                        dve.sem_inc(s_S, 1)

                @sweep
                def run(i, q, ahead, make, inv, rec):
                    j = i + 1
                    for l in range(LV):
                        if inv:
                            for p in range(2):
                                level(j, l, p)
                        if rec:
                            recur(i, q, l // 3, l % 3)
                        if inv:
                            for p in range(2):
                                level_x(j, l, p)
                        if make and l % 3 == 0:
                            scores(i + 2, q, l // 3)
                        if make and l % 3 == 1:
                            first(i + 2, q, l // 3)
                    if inv:
                        for p in range(2):
                            newton(j, p)
                run(dve)


def pipeline(eng, count, *steps):
    def turn(i, j=None):
        for lead, stage in steps:
            t = i + lead
            if j is not None:
                stage(t, (j + lead) % 2, 0, False)
            elif 0 <= t < count:
                stage(t, t % 2, 1 if t < CCH else 0, t < 2)
    for i in range(-2, 4):
        turn(i)
    with eng.Fori(2, count // 2 - 1) as pair:
        for j in range(2):
            turn(pair * 2 + j, j)
    for i in range(count - 2, count + 1):
        turn(i)


def is_first(i):
    return isinstance(i, int) and i == 0


def gate_rows(pe, coef, layer, w, ident, banks, sem_done):
    for k in range(KT):
        m = pe.matmul(banks[k // 4][:, (k % 4) * P:(k % 4 + 1) * P],
                      coef[:, layer, 2, w, k:k + 1].broadcast_to([P, P]), ident[:], start=True, stop=True)
    m.then_inc(sem_done, 1)


def split_weights(nc, eng_name, eng, rows, stage, whi, wlo, s_hi, s_lo, w_load):
    for k in range(rows):
        if eng_name == "act":
            eng.wait_ge(w_load[k % 4], 16 * (k // 4 + 1))
            eng.activation(whi[:, k, :], stage[k % 4], ACT.Copy).then_inc(s_hi, 1)
        elif k % 2 == (eng_name == "dve"):
            eng.wait_ge(s_hi, k + 1)
            eng.tensor_tensor(wlo[:, k, :], stage[k % 4], whi[:, k, :].bitcast(F32), ALU.subtract).then_inc(s_lo[k % 2], 1)


def load_weights(sp, rows, stage, src, s_lo, w_load):
    for k in range(rows):
        if k >= 4:
            sp.wait_ge(s_lo[k % 2], k // 2 - 1)
        sp.dma_start(stage[k % 4], src[k * P:(k + 1) * P, :]).then_inc(w_load[k % 4], 16)


def phase_output_gdn(nc, sem, T, io, dram):
    with ExitStack() as ctx:
        sb = lambda x, s, d=F32: ctx.enter_context(nc.sbuf_tensor("og_" + x, s, d))
        two = lambda x, s, d=F32: [sb(f"{x}{j}", s, d) for j in range(2)]
        whi, wlo = sb("whi", [P, NV, D], F32R), sb("wlo", [P, NV, D], F32R)
        gate = sb("gate", [P, 2, D])
        of, ob = sb("of", [P, NV, P]), sb("ob", [P, NV, P])
        z = sb("z", [P, NV, P])
        hi, lo = two("hi", [P, NV, P], F32R), two("lo", [P, NV, P], F32R)
        xt = two("x", [P, D])
        y = sb("y", [P, D])
        ss = two("ss", [P, NV])
        tp = [ctx.enter_context(nc.psum_tensor(f"og_tp{i}", [P, 512], F32)) for i in range(4)]
        yp = [[ctx.enter_context(nc.psum_tensor(f"og_y{j}{i}", [P, 512], F32)) for i in range(2)] for j in range(2)]
        stage = [z[:].rearrange("p a b -> p (a b)")[:, k * D:(k + 1) * D] for k in range(2)] + [xt[k][:] for k in range(2)]
        names = ("w_hi", "gate", "gate_read", "add", "square", "sum", "root", "recip", "scaled",
                 "turned", "load_z", "oT", "hi", "lo", "y", "gated", "final", "turn")
        s = {q: sem("og_" + q) for q in names}
        w_load = [sem(f"og_w_load{j}") for j in range(4)]
        w_lo, load_o, load_x, stored = ([sem(f"og_{x}{j}") for j in range(2)]
                                                for x in ("w_lo", "load_o", "load_x", "stored"))
        with nc.Block() as block:
            @block.sync
            def _(sp):
                def loads_o(i, j, w, first):
                    c = known(sp, i * 1 + 0)
                    if not is_first(i):
                        sp.wait_ge(s["turned"], i)
                        settle(sp, s["turn"])
                        sp.wait_ge(s["sum"], i)
                        settle(sp, s["turn"])
                    for d, buf in enumerate((of, ob)):
                        sp.dma_start(buf[:], dram["o"][d, bass.ds(c, 1)].rearrange("o p n t -> (o p) n t")).then_inc(load_o[j], 16)

                def load_zp(i, j, w, first):
                    c = known(sp, i * 1 + 0)
                    if not is_first(i):
                        sp.wait_ge(s["lo"], i)
                        settle(sp, s["turn"])
                    sp.dma_start(z[:], dram["z"][bass.ds(c, 1)].rearrange("o p n t -> (o p) n t")).then_inc(s["load_z"], 16)

                def store(i, j, w, first):
                    c = known(sp, i * 1 + 0)
                    sp.wait_ge(s["final"], i + 1)
                    settle(sp, s["turn"])
                    sp.dma_start(dram["tokens1"][bass.ds(c * P, P), :], xt[j][:]).then_inc(stored[j], 16)

                def load_res(i, j, w, first):
                    c = known(sp, i * 1 + 0)
                    if not first:
                        sp.wait_ge(stored[j], (i - j) * 8)
                        settle(sp, s["turn"])
                    sp.dma_start(xt[j][:], io["tokens"][bass.ds(c * P, P), :]).then_inc(load_x[j], 16)

                load_weights(sp, NV, stage, io["gdn_w_out"], w_lo, w_load)

                def load_z_after_weights(i, j, w, first):
                    if is_first(i):
                        for m in range(2):
                            sp.wait_ge(w_lo[m], NV // 2)
                    load_zp(i, j, w, first)
                pipeline(sp, NCH, (1, loads_o), (1, load_z_after_weights), (0, load_res), (-1, store))
                for j in range(2):
                    sp.wait_ge(stored[j], 8 * NCH)

            @block.gpsimd
            def _(pool):
                split_weights(nc, "pool", pool, NV, stage, whi, wlo, s["w_hi"], w_lo, w_load)

                def scale(i, j, w, first):
                    pool.wait_ge(s["recip"], i + 1)
                    pool.tensor_tensor(of[:], of[:], ss[j][:].unsqueeze(2).broadcast_to([P, NV, P]), ALU.mult
                                       ).then_inc(s["scaled"], 1)
                pipeline(pool, NCH, (1, scale))

            @block.scalar
            def _(act):
                split_weights(nc, "act", act, NV, stage, whi, wlo, s["w_hi"], w_lo, w_load)

                def high(i, j, w, first):
                    act.wait_ge(s["oT"], i + 1)
                    if not first:
                        act.wait_ge(s["y"], i - 1)
                    act.activation(hi[j][:], z[:], ACT.Copy).then_inc(s["hi"], 1)

                def norms(i, j, w, first):
                    act.wait_ge(s["add"], i + 1)
                    act.activation(ob[:], of[:], ACT.Square).then_inc(s["square"], 1)
                    act.wait_ge(s["sum"], i + 1)
                    act.activation(ss[j][:], ss[j][:], ACT.Sqrt, bias=T["eps"][:], scale=1.0 / HD).then_inc(s["root"], 1)
                pipeline(act, NCH, (0, high), (1, norms))

            @block.tensor
            def _(pe):
                for w in range(2):
                    gate_rows(pe, T["coef"], 0, w, T["ident"], yp[w], s["gate"])
                pe.wait_ge(s["gate_read"], 2)

                def turn(i, j, w, first):
                    pe.wait_ge(s["scaled"], i + 1)
                    if not is_first(i):
                        pe.wait_ge(s["oT"], i)
                    for n in range(NV):
                        t = pe.transpose(tp[n // 4][:, (n % 4) * P:(n % 4 + 1) * P], of[:, n, :], T["ident"][:])
                    t.then_inc(s["turned"], 1)

                def products(i, j, w, first):
                    pe.wait_ge(s["lo"], i + 1)
                    if not first:
                        pe.wait_ge(s["gated"], i - 1)
                    for half in range(2):
                        m = 0
                        for l, r in ((hi, whi), (hi, wlo), (lo, whi)):
                            for k in range(NV):
                                t = pe.matmul(yp[j][half][:], l[j][:, k, :], r[:, k, half * 512:(half + 1) * 512],
                                              start=(m == 0), stop=(m == 3 * NV - 1))
                                m += 1
                    t.then_inc(s["y"], 1)
                pipeline(pe, NCH, (0, turn), (-1, products))

            @block.vector
            def _(dve):
                for w in range(2):
                    dve.wait_ge(s["gate"], w + 1)
                    for half in range(2):
                        t = dve.tensor_copy(gate[:, w, half * 512:(half + 1) * 512], yp[w][half][:])
                    t.then_inc(s["gate_read"], 1)
                split_weights(nc, "dve", dve, NV, stage, whi, wlo, s["w_hi"], w_lo, w_load)

                def turned(i, j, w, first):
                    dve.wait_ge(s["turned"], i + 1)
                    dve.wait_ge(s["load_z"], i * 16 + 16)
                    for b in range(4):
                        v = z[:, 4 * b:4 * b + 4].rearrange("p a t -> p (a t)")
                        t = dve.tensor_tensor(v, tp[b][:], v, ALU.mult)
                    t.then_inc(s["oT"], 1)

                def add(i, j, w, first):
                    dve.wait_ge(load_o[j], (i - j) * 16 + 32)
                    dve.tensor_tensor(of[:], of[:], ob[:], ALU.add).then_inc(s["add"], 1)

                def low(i, j, w, first):
                    dve.wait_ge(s["hi"], i + 1)
                    if not first:
                        dve.wait_ge(s["y"], i - 1)
                    dve.tensor_tensor(lo[j][:], z[:], hi[j][:].bitcast(F32), ALU.subtract).then_inc(s["lo"], 1)

                def norms(i, j, w, first):
                    dve.wait_ge(s["square"], i + 1)
                    if not first:
                        dve.wait_ge(s["scaled"], i - 1)
                    dve.reduce_sum(ss[j][:], ob[:], AX.X).then_inc(s["sum"], 1)
                    dve.wait_ge(s["root"], i + 1)
                    dve.reciprocal(ss[j][:], ss[j][:]).then_inc(s["recip"], 1)

                def residual(i, j, w, first):
                    dve.wait_ge(s["y"], i + 1)
                    if not is_first(i):
                        dve.wait_ge(s["final"], i)
                    for half in range(2):
                        h = slice(half * 512, (half + 1) * 512)
                        t = dve.tensor_tensor(y[:, h], yp[j][half][:], gate[:, w, h], ALU.mult)
                    t.then_inc(s["gated"], 1)
                    dve.wait_ge(s["gated"], i + 1)
                    dve.wait_ge(load_x[j], (i - j) * 8 + 16)
                    dve.tensor_tensor(xt[j][:], xt[j][:], y[:], ALU.add).then_inc(s["final"], 1)
                pipeline(dve, NCH, (0, turned), (1, add), (0, low), (1, norms), (-1, residual))


def phase_project_lru(nc, sem, T, io, dram, hi, lo):
    with ExitStack() as ctx:
        sb = lambda x, s, d=F32: ctx.enter_context(nc.sbuf_tensor("pl_" + x, s, d))
        NT = 2
        pr = Projection(nc, sem, ctx, T, "pl_", io["lru_w_in"][0], hi, lo, [0, D], [P, P])
        raw = [sb(f"raw{j}", [P, RAW]) for j in range(2)]
        acc = [sb(f"acc{j}", [P, CONV]) for j in range(2)]
        cw, cb = sb("conv_w", [P, 4, KT]), sb("conv_b", [P, KT])
        names = ("const", "pads", "conv0", "conv1", "conv2", "ready0", "ready1", "turn")
        s = {q: sem("pl_" + q) for q in names}
        stored = [sem(f"pl_stored{j}") for j in range(2)]

        def sweep(eng, stage):
            for j in range(NT):
                stage(0, j, True)
            with eng.Fori(1, KT) as h:
                for j in range(NT):
                    stage(h, j, False)

        with nc.Block() as block:
            @block.sync
            def _(sp):
                sp.dma_start(cw[:], io["lru_conv_w"]).then_inc(s["const"], 16)
                sp.dma_start(cb[:], io["lru_conv_b"]).then_inc(s["const"], 16)
                for j in range(NT):
                    pr.load(sp, 0, j, True)

                def stage(h, j, more):
                    if more:
                        pr.load(sp, h + 1, j, False)
                    row = known(sp, h * 1 + 0)
                    sp.wait_ge(s[f"ready{j}"], h + 1)
                    settle(sp, s["turn"])
                    dst = dram["xc" if j == 0 else "gate1"][bass.ds(row, 1)].rearrange("o p t -> (o p) t")
                    for d, src in zip((dst[:, 0:CTX], dst[:, CTX:TOK]), sequences(acc[j])):
                        sp.dma_start(d, src).then_inc(stored[j], 16)
                for j in range(NT):
                    stage(0, j, True)
                with sp.Fori(1, KT - 1) as h:
                    for j in range(NT):
                        stage(h, j, True)
                for j in range(NT):
                    stage(KT - 1, j, False)
                for j in range(NT):
                    sp.wait_ge(stored[j], 32 * KT)

            @block.gpsimd
            def _(pool):
                sweep(pool, lambda h, j, first: pr.split(pool, h, j, first))

            @block.tensor
            def _(pe):
                def stage(h, j, first):
                    for blk in range(NB):
                        pr.products(pe, h, j, blk, first and j == 0)
                sweep(pe, stage)

            @block.scalar
            def _(act):
                act.wait_ge(s["pads"], 2)

                def stage(h, j, first):
                    for blk in range(NB):
                        act.wait_ge(pr.s_mm, (h * NT + j) * NB + blk + 1)
                        if blk == 0 and not first:
                            act.wait_ge(s[f"ready{j}"], h)
                        act.activation(raw_row(raw[j], blk), pr.bank[blk][:, 0:BLKS[blk][1]],
                                       ACT.Silu if j else ACT.Copy).then_inc(pr.s_ev, 1)
                sweep(act, stage)

            @block.vector
            def _(dve):
                for j in range(NT):
                    dve.memset(raw[j][:], 0.0).then_inc(s["pads"], 1)
                dve.wait_ge(s["const"], 32)

                def stage(h, j, first):
                    dve.wait_ge(pr.s_ev, (h * NT + j) * NB + NB)
                    if not first:
                        dve.wait_ge(stored[j], h * 32)
                    if j:
                        dve.tensor_copy(acc[j][:], raw[j][:, PAD_L:PAD_L + CONV]).then_inc(s["ready1"], 1)
                        return
                    tap = lambda m: cw[:, m, bass.ds(h, 1)]
                    dve.tensor_scalar(acc[j][:], raw[j][:, 0:CONV], tap(0), cb[:, bass.ds(h, 1)], ALU.mult, ALU.add
                                      ).then_inc(s["conv0"], 1)
                    for m in (1, 2, 3):
                        dve.wait_ge(s[f"conv{m - 1}"], h + 1)
                        dve.scalar_tensor_tensor(acc[j][:], raw[j][:, m:m + CONV], tap(m), acc[j][:], ALU.mult, ALU.add
                                                 ).then_inc(s[f"conv{m}"] if m < 3 else s["ready0"], 1)
                sweep(dve, stage)


def phase_scan(nc, sem, T, io, dram):
    S2 = 2
    NU = 2 * S2 * LB
    with ExitStack() as ctx:
        sb = lambda x, s, d=F32: ctx.enter_context(nc.sbuf_tensor("sc_" + x, s, d))
        two = lambda x, s, d=F32: [sb(f"{x}{j}", s, d) for j in range(2)]
        w32 = sb("w32", [P, 2, 2, 2, 256])
        whi, wlo = sb("whi", [P, 2, 2, 2, 256], F32R), sb("wlo", [P, 2, 2, 2, 256], F32R)
        xc = two("xc", [P, S2, TOK])
        xhi, xlo = sb("xhi", [P, S2, TOK], F32R), sb("xlo", [P, S2, TOK], F32R)
        gate, mixed = sb("gate", [P, SEQ]), sb("mixed", [P, SEQ])
        A, I, Tn, H = two("A", [P, TOK]), two("I", [P, TOK]), two("T", [P, TOK]), two("H", [P, TOK])
        V = sb("V", [P, TOK])
        br, bi = sb("br", [P, 2, KT]), sb("bi", [P, 2, KT])
        lam, c8, nc8 = sb("lam", [P, 2, KT]), sb("c8", [P, 2, KT]), sb("nc8", [P, 2, KT])
        tl = sb("tl", [P, 2, KT])
        bank = [ctx.enter_context(nc.psum_tensor(f"sc_b{i}", [P, 512], F32)) for i in range(8)]
        names = ("const", "la", "le", "ln", "lp", "lq", "nc8", "w_hi", "w_lo", "x_hi", "x_lo0", "x_lo1", "mm", "ev", "tanh",
                 "a", "sq", "v", "root", "ix", "b", "scan", "ctx_scan", "sum", "mix", "gate_load", "stored")
        s = {q: sem("sc_" + q) for q in names}
        load_w, load_x = ([sem(f"sc_{x}{j}") for j in range(2)] for x in ("load_w", "load_x"))
        GR = [(g, blk) for g in range(2) for blk in range(NB)]
        NG = len(GR)
        units = [(u, u // 4, u // 2 % 2, u % 2) for u in range(NU)]

        with nc.Block() as block:
            @block.sync
            def _(sp):
                def block_loads(b):
                    if b >= 1:
                        sp.wait_ge(s["w_lo"], b)
                    for d in range(2):
                        for g, w in enumerate(("lru_w_r", "lru_w_i")):
                            sp.dma_start(w32[:, d, g], io[w][d][b].rearrange("(k p) n -> p k n", p=P)).then_inc(load_w[b % 2], 16)
                    if b >= 2:
                        sp.wait_ge(s["ix"], 4 * (b - 1))
                        sp.wait_ge(s["x_lo0"], b - 1)
                        sp.wait_ge(s["x_lo1"], b - 1)
                    sp.dma_start(xc[b % 2][:], dram["xc"][2 * b:2 * b + 2].rearrange("s p t -> p s t")).then_inc(load_x[b % 2], 16)

                def gate_load(k):
                    sp.dma_start(gate[:], dram["gate1"][k][:, CTX:TOK]).then_inc(s["gate_load"], 16)

                block_loads(0)
                for dst, src in ((br, "lru_b_r"), (bi, "lru_b_i"), (lam, "lru_lambda")):
                    sp.dma_start(dst[:], io[src]).then_inc(s["const"], 16)
                gate_load(0)
                block_loads(1)
                for k in range(KT):
                    sp.wait_ge(s["mix"], k + 1)
                    sp.dma_start(dram["mixed"][k], mixed[:]).then_inc(s["stored"], 16)
                    if k + 1 < KT:
                        gate_load(k + 1)
                    if k % 2 and k // 2 + 2 < LB:
                        block_loads(k // 2 + 2)
                sp.wait_ge(s["stored"], 16 * KT)

            @block.gpsimd
            def _(pool):
                def split(b):
                    pool.wait_ge(s["x_hi"], 2 * b + 1)
                    pool.tensor_tensor(xlo[:, 0], xc[b % 2][:, 0], xhi[:, 0].bitcast(F32), ALU.subtract).then_inc(s["x_lo0"], 1)
                split(0)
                for u, b, t, d in units:
                    pool.wait_ge(s["ev"], (u + 1) * NG)
                    pool.tensor_tensor(I[d][:], I[d][:], xc[b % 2][:, t], ALU.mult).then_inc(s["ix"], 1)
                    if u % 4 == 3 and b + 1 < LB:
                        split(b + 1)

            @block.tensor
            def _(pe):
                def one(b, first):
                    pe.wait_ge(s["w_lo"], b + 1)
                    pe.wait_ge(s["x_lo0"], b + 1)
                    pe.wait_ge(s["x_lo1"], b + 1)
                    n = 0
                    for t in range(S2):
                        for d in range(2):
                            for g, blk in GR:
                                if not (first and n < 8):
                                    pe.wait_ge(s["ev"], b * (4 * NG) + n - 7)
                                at, w = BLKS[blk]
                                m = 0
                                for l, r in ((whi, xhi), (whi, xlo), (wlo, xhi)):
                                    for k in range(2):
                                        i = pe.matmul(bank[n % 8][:, 0:w], l[:, d, g, k, t * P:(t + 1) * P], r[:, k, at:at + w],
                                                      start=(m == 0), stop=(m == 5))
                                        m += 1
                                i.then_inc(s["mm"], 1)
                                n += 1
                assert 4 * NG % 8 == 0
                one(0, True)
                with pe.Fori(1, LB) as b:
                    one(b, False)

            @block.scalar
            def _(act):
                def split(b):
                    if b:
                        act.wait_ge(s["mm"], b * (4 * NG))
                    act.wait_ge(load_w[b % 2], 64 * (b // 2 + 1))
                    act.activation(whi[:], w32[:], ACT.Copy).then_inc(s["w_hi"], 1)
                    act.wait_ge(load_x[b % 2], 16 * (b // 2 + 1))
                    for k in range(2):
                        act.activation(xhi[:, k], xc[b % 2][:, k], ACT.Copy).then_inc(s["x_hi"], 1)
                split(0)
                act.wait_ge(s["const"], 48)
                act.activation(tl[:], lam[:], ACT.Abs).then_inc(s["la"], 1)
                act.wait_ge(s["la"], 1)
                act.activation(tl[:], tl[:], ACT.Exp, scale=-1.0).then_inc(s["le"], 1)
                act.wait_ge(s["le"], 1)
                act.activation(tl[:], tl[:], ACT.Ln, bias=1.0).then_inc(s["ln"], 1)
                act.wait_ge(s["nc8"], 1)

                def root(u):
                    act.wait_ge(s["v"], u + 1)
                    act.activation(Tn[u % 2][:], Tn[u % 2][:], ACT.Sqrt).then_inc(s["root"], 1)

                for u, b, t, d in units:
                    if u >= 2:
                        act.wait_ge(s["scan"], u - 1)
                    for n, (g, blk) in enumerate(GR):
                        at, w = BLKS[blk]
                        act.wait_ge(s["mm"], u * NG + n + 1)
                        act.activation((I if g else A)[d][:, at:at + w], bank[(u * NG + n) % 8][:, 0:w], ACT.Sigmoid,
                                       bias=(bi if g else br)[:, d, 2 * b + t:2 * b + t + 1]).then_inc(s["ev"], 1)
                    if u % 4 == 3 and b + 1 < LB:
                        split(b + 1)
                    if u:
                        root(u - 1)
                    act.wait_ge(s["ev"], (u + 1) * NG)
                    act.activation(Tn[d][:], A[d][:], ACT.Tanh, scale=c8[:, d, 2 * b + t:2 * b + t + 1]).then_inc(s["tanh"], 1)
                    act.wait_ge(s["tanh"], u + 1)
                    act.activation(A[d][:], A[d][:], ACT.Exp, scale=nc8[:, d, 2 * b + t:2 * b + t + 1]).then_inc(s["a"], 1)
                root(NU - 1)

            @block.vector
            def _(dve):
                def split(b):
                    dve.wait_ge(s["w_hi"], b + 1)
                    dve.tensor_tensor(wlo[:], w32[:], whi[:].bitcast(F32), ALU.subtract).then_inc(s["w_lo"], 1)
                    dve.wait_ge(s["x_hi"], 2 * b + 2)
                    dve.tensor_tensor(xlo[:, 1], xc[b % 2][:, 1], xhi[:, 1].bitcast(F32), ALU.subtract).then_inc(s["x_lo1"], 1)
                split(0)
                dve.wait_ge(s["ln"], 1)
                dve.tensor_scalar(lam[:], lam[:], -1.0, 0.0, ALU.mult, ALU.max).then_inc(s["lp"], 1)
                dve.wait_ge(s["lp"], 1)
                dve.tensor_tensor(lam[:], lam[:], tl[:], ALU.add).then_inc(s["lq"], 1)
                dve.wait_ge(s["lq"], 1)
                dve.tensor_scalar(c8[:], lam[:], RG_C, None, ALU.mult)
                dve.tensor_scalar(nc8[:], lam[:], -RG_C, None, ALU.mult).then_inc(s["nc8"], 1)

                def scan(u, d):
                    dve.wait_ge(s["root"], u + 1)
                    dve.wait_ge(s["ix"], u + 1)
                    dve.tensor_tensor(I[d][:], Tn[d][:], I[d][:], ALU.mult).then_inc(s["b"], 1)
                    dve.wait_ge(s["b"], u + 1)
                    if u >= 2:
                        dve.wait_ge(s["mix"], u // 2)
                    turn = lambda v: v if d == 0 else v[:, ::-1]
                    edge = CTX - 1 if d == 0 else 0
                    for sl, start, done in ((slice(0, CTX), 0.0, "ctx_scan"), (slice(CTX, TOK), H[d][:, edge:edge + 1], "scan")):
                        dve.tensor_tensor_scan(turn(H[d][:, sl]), turn(A[d][:, sl]), turn(I[d][:, sl]), start,
                                               ALU.mult, ALU.add).then_inc(s[done], 1)
                        dve.wait_ge(s[done], u + 1)

                def mix(k):
                    dve.tensor_tensor(H[0][:, CTX:TOK], H[0][:, CTX:TOK], H[1][:, CTX:TOK], ALU.add).then_inc(s["sum"], 1)
                    dve.wait_ge(s["sum"], k + 1)
                    dve.wait_ge(s["gate_load"], 16 * (k + 1))
                    if k:
                        dve.wait_ge(s["stored"], 16 * k)
                    dve.tensor_tensor(mixed[:].rearrange("p (r c) -> p c r", c=GRID_W),
                                      H[0][:, CTX:TOK].rearrange("p (c r) -> p c r", r=ROWS),
                                      gate[:].rearrange("p (c r) -> p c r", r=ROWS), ALU.mult).then_inc(s["mix"], 1)
                for u, b, t, d in units:
                    if u:
                        scan(u - 1, 1 - d)
                    dve.wait_ge(s["a"], u + 1)
                    dve.tensor_tensor(V[:], A[d][:], A[d][:], ALU.mult).then_inc(s["sq"], 1)
                    dve.wait_ge(s["sq"], u + 1)
                    dve.wait_ge(s["tanh"], u + 1)
                    dve.scalar_tensor_tensor(Tn[d][:], V[:], 1.0, Tn[d][:], ALU.add, ALU.mult).then_inc(s["v"], 1)
                    if u and d == 0:
                        mix(u // 2 - 1)
                    if u % 4 == 2 and b + 1 < LB:
                        split(b + 1)
                scan(NU - 1, 1)
                mix(KT - 1)


def phase_output_lru(nc, sem, T, io, dram, out):
    NTL = SEQ // P
    with ExitStack() as ctx:
        sb = lambda x, s, d=F32: ctx.enter_context(nc.sbuf_tensor("ol_" + x, s, d))
        two = lambda x, s, d=F32: [sb(f"{x}{j}", s, d) for j in range(2)]
        w32 = sb("w32", [P, 4, D])
        whi, wlo = sb("whi", [P, KT, D], F32R), sb("wlo", [P, KT, D], F32R)
        gate, fg = sb("gate", [P, D]), sb("final_g", [P, D])
        mx, xt, y = two("mix", [P, KT, P]), two("x", [P, D]), two("y", [P, D])
        hi, lo = two("hi", [P, KT, P], F32R), two("lo", [P, KT, P], F32R)
        ss, rs = two("ss", [P, 1]), two("rs", [P, 1])
        yp = [[ctx.enter_context(nc.psum_tensor(f"ol_y{j}{i}", [P, 512], F32)) for i in range(2)] for j in range(2)]
        gp = [ctx.enter_context(nc.psum_tensor(f"ol_g{i}", [P, 512], F32)) for i in range(2)]
        names = ("const", "w_hi", "gate", "gate_read", "hi", "lo", "y", "gated", "res", "sum", "root", "recip", "final", "turn")
        s = {q: sem("ol_" + q) for q in names}
        w_load = [sem(f"ol_w_load{j}") for j in range(4)]
        w_lo, load_m, load_x, stored = ([sem(f"ol_{x}{j}") for j in range(2)] for x in ("w_lo", "load_m", "load_x", "stored"))
        stage = [w32[:, k, :] for k in range(4)]

        with nc.Block() as block:
            @block.sync
            def _(sp):
                load_weights(sp, KT, stage, io["lru_w_out"], w_lo, w_load)
                sp.dma_start(fg[:], io["final_g"].partition_broadcast(P)).then_inc(s["const"], 16)

                def load_mix(i, j, w, first):
                    at = known(sp, i * P)
                    if not first:
                        sp.wait_ge(s["lo"], i - 1)
                        settle(sp, s["turn"])
                    sp.dma_start(mx[j][:], dram["mixed"].rearrange("k p t -> p k t")[:, :, bass.ds(at, P)]).then_inc(load_m[j], 16)

                def load_res(i, j, w, first):
                    at = known(sp, i * P)
                    if not first:
                        sp.wait_ge(s["final"], i - 1)
                        settle(sp, s["turn"])
                    sp.dma_start(xt[j][:], dram["tokens1"][bass.ds(at + CTX, P), :]).then_inc(load_x[j], 16)

                def store(i, j, w, first):
                    at = known(sp, i * P)
                    sp.wait_ge(s["final"], i + 1)
                    settle(sp, s["turn"])
                    sp.dma_start(out[bass.ds(at, P), :], y[j][:]).then_inc(stored[j], 16)
                pipeline(sp, NTL, (2, load_mix), (-1, store), (1, load_res))
                for j in range(2):
                    sp.wait_ge(stored[j], 8 * NTL)

            @block.gpsimd
            def _(pool):
                split_weights(nc, "pool", pool, KT, stage, whi, wlo, s["w_hi"], w_lo, w_load)

                def low(i, j, w, first):
                    pool.wait_ge(s["hi"], i + 1)
                    if not first:
                        pool.wait_ge(s["y"], i - 1)
                    pool.tensor_tensor(lo[j][:], mx[j][:], hi[j][:].bitcast(F32), ALU.subtract).then_inc(s["lo"], 1)
                pipeline(pool, NTL, (1, low))

            @block.scalar
            def _(act):
                split_weights(nc, "act", act, KT, stage, whi, wlo, s["w_hi"], w_lo, w_load)

                def high(i, j, w, first):
                    act.wait_ge(load_m[j], (i - j) * 8 + 16)
                    if not first:
                        act.wait_ge(s["y"], i - 1)
                    act.activation(hi[j][:], mx[j][:], ACT.Copy).then_inc(s["hi"], 1)

                def norm(i, j, w, first):
                    act.wait_ge(s["res"], i + 1)
                    act.activation(y[j][:], xt[j][:], ACT.Square, accum_out=ss[j][:]).then_inc(s["sum"], 1)
                    act.wait_ge(s["sum"], i + 1)
                    act.activation(ss[j][:], ss[j][:], ACT.Sqrt, bias=T["eps"][:], scale=1.0 / D).then_inc(s["root"], 1)
                pipeline(act, NTL, (1, high), (-1, norm))

            @block.tensor
            def _(pe):
                gate_rows(pe, T["coef"], 1, 0, T["ident"], gp, s["gate"])

                def products(i, j, w, first):
                    if is_first(i):
                        for m in range(2):
                            pe.wait_ge(w_lo[m], KT // 2)
                    pe.wait_ge(s["lo"], i + 1)
                    if not first:
                        pe.wait_ge(s["gated"], i - 1)
                    for half in range(2):
                        m = 0
                        for l, r in ((hi, whi), (hi, wlo), (lo, whi)):
                            for k in range(KT):
                                t = pe.matmul(yp[j][half][:], l[j][:, k, :], r[:, k, half * 512:(half + 1) * 512],
                                              start=(m == 0), stop=(m == 3 * KT - 1))
                                m += 1
                    t.then_inc(s["y"], 1)
                pipeline(pe, NTL, (0, products))

            @block.vector
            def _(dve):
                dve.wait_ge(s["gate"], 1)
                for half in range(2):
                    t = dve.tensor_copy(gate[:, half * 512:(half + 1) * 512], gp[half][:])
                t.then_inc(s["gate_read"], 1)
                split_weights(nc, "dve", dve, KT, stage, whi, wlo, s["w_hi"], w_lo, w_load)
                dve.wait_ge(s["gate_read"], 1)
                dve.wait_ge(s["const"], 16)

                def residual(i, j, w, first):
                    dve.wait_ge(s["y"], i + 1)
                    if not first:
                        dve.wait_ge(stored[j], (i - j) * 8)
                    for half in range(2):
                        h = slice(half * 512, (half + 1) * 512)
                        t = dve.tensor_tensor(y[j][:, h], yp[j][half][:], gate[:, h], ALU.mult)
                    t.then_inc(s["gated"], 1)
                    dve.wait_ge(s["gated"], i + 1)
                    dve.wait_ge(load_x[j], (i - j) * 8 + 16)
                    dve.tensor_tensor(xt[j][:], xt[j][:], y[j][:], ALU.add).then_inc(s["res"], 1)

                def final(i, j, w, first):
                    dve.wait_ge(s["root"], i + 1)
                    dve.reciprocal(rs[j][:], ss[j][:]).then_inc(s["recip"], 1)
                    dve.wait_ge(s["recip"], i + 1)
                    dve.scalar_tensor_tensor(y[j][:], xt[j][:], rs[j][:], fg[:], ALU.mult, ALU.mult).then_inc(s["final"], 1)
                pipeline(dve, NTL, (0, residual), (-1, final))


def build(nc, io, dram, out):
    with ExitStack() as ctx:
        taken = []

        def sem(name):
            taken.append(nc.alloc_semaphore(name))
            return taken[-1]

        def reuse_semaphores():
            nc.clear_and_free_semaphores(taken)
            taken.clear()
            nc.all_engine_barrier()

        T = {
            "ident": ctx.enter_context(nc.sbuf_tensor("ident", [P, P], F32)),
            "ones": ctx.enter_context(nc.sbuf_tensor("ones", [P, P], F32)),
            "coef": ctx.enter_context(nc.sbuf_tensor("coef", [P, 2, 3, 2, KT], F32)),
            "eps": ctx.enter_context(nc.sbuf_tensor("eps_col", [P, 1], F32)),
        }
        phase_modulation(nc, sem, T, io)
        with ExitStack() as c2:
            hi = c2.enter_context(nc.sbuf_tensor("h0_hi", [P, KT, TOK], F32R))
            lo = c2.enter_context(nc.sbuf_tensor("h0_lo", [P, KT, TOK], F32R))
            phase_norm(nc, sem, T, 0, io["tokens"], hi, lo, False)
            phase_gates(nc, sem, T, io, dram, hi, lo)
            phase_project_gdn(nc, sem, T, io, dram, hi, lo)
        phase_delta_core(nc, sem, T, io, dram)
        reuse_semaphores()
        phase_output_gdn(nc, sem, T, io, dram)
        with ExitStack() as c2:
            hi = c2.enter_context(nc.sbuf_tensor("h1_hi", [P, KT, TOK], F32R))
            lo = c2.enter_context(nc.sbuf_tensor("h1_lo", [P, KT, TOK], F32R))
            phase_norm(nc, sem, T, 1, dram["tokens1"], hi, lo, True)
            phase_project_lru(nc, sem, T, io, dram, hi, lo)
        phase_scan(nc, sem, T, io, dram)
        phase_output_lru(nc, sem, T, io, dram, out)


def kernel(**inputs):
    import concourse.bacc as bacc
    from concourse.bass_utils import run_bass_kernel_spmd

    nc = bacc.Bacc("TRN2", target_bir_lowering=False, num_devices=1)
    a = {k: np.asarray(v) for k, v in inputs.items()}
    cols = lambda v: np.ascontiguousarray(np.moveaxis(v.reshape(v.shape[:-1] + (-1, P)), -1, 0))
    i, j = np.arange(P)[:, None], np.arange(P)[None, :]
    lev = np.zeros((P, NLEV, 2, P), np.float16)
    for n in range(NLEV):
        s = 1 << n
        pair = (i // (2 * s) == j // (2 * s))
        up = pair & (i // s % 2 == 0) & (j // s % 2 == 1)
        lev[:, n, 0], lev[:, n, 1] = -1.0 * up, -1.0 * up.T
    arrays = {
        "tokens": np.concatenate([a["ctx"][0], a["x"][0]], 0),
        "cvec": np.ascontiguousarray(np.stack([cols(a["c"][0]), cols(a["c_ctx"])], -1)),
        "mod_w": a["mod_w"], "mod_b": cols(a["mod_b"]), "norm_g": cols(a["norm_g"]),
        "final_g": a["final_g"],
        "gdn_w_in": a["gdn_w_in"], "gdn_conv": cols(a["gdn_conv"][0]),
        "gdn_a_log": a["gdn_a_log"].reshape(-1), "gdn_dt_bias": a["gdn_dt_bias"].reshape(-1),
        "gdn_norm_g": a["gdn_norm_g"].reshape(P, 1), "gdn_w_out": a["gdn_w_out"][0],
        "lru_w_in": a["lru_w_in"], "lru_conv_w": cols(a["lru_conv_w"][0]), "lru_conv_b": cols(a["lru_conv_b"][0]),
        "lru_w_r": a["lru_w_r"][0], "lru_b_r": cols(a["lru_b_r"][0]), "lru_w_i": a["lru_w_i"][0],
        "lru_b_i": cols(a["lru_b_i"][0]), "lru_lambda": cols(a["lru_lambda"][0]), "lru_w_out": a["lru_w_out"][0],
        "ident": np.eye(P, dtype=np.float32), "ident16": np.tile(np.eye(P, dtype=np.float16), (1, 4)),
        "tri": np.stack([i <= j, i >= j], 1).astype(np.float32),
        "incl": np.stack([i <= j, i >= j], 1).astype(np.float32),
        "strict": np.stack([i > j, i < j], 1).astype(np.float32),
        "levels": lev,
    }
    io = {k: nc.dram_tensor("in_" + k, v.shape, mybir.dt.from_np(v.dtype), kind="ExternalInput").ap()
          for k, v in arrays.items()}
    scratch = {
        "gates": (NCH, P, NQ * 2 * NQTY * 2), "cgrow": (2 * NV, TOK),
        "fm": (NQ, NCH, P, 2, P), "tm": (NQ, NCH, P, 3, P), "z": (NCH, P, NV, P),
        "o": (2, NCH, P, NV, P), "tokens1": (TOK, D),
        "xc": (KT, P, TOK), "gate1": (KT, P, TOK), "mixed": (KT, P, SEQ),
    }
    dram = {k: nc.dram_tensor("scratch_" + k, v, F32, kind="Internal").ap() for k, v in scratch.items()}
    out = nc.dram_tensor("out", (SEQ, D), F32, kind="ExternalOutput").ap()
    build(nc, io, dram, out)
    r = run_bass_kernel_spmd(nc, [{"in_" + k: v for k, v in arrays.items()}], core_ids=[0])
    return r.results[0]["out"].reshape(1, SEQ, D)
```
